# Optimizing a Trainium2 kernel written in Bass

```python
import jax, jax.numpy as jnp
from jax import lax
import numpy as np

D_MODEL = 1024
BATCH = 1
SEQ = 512
DEPTH = 1

MIX_WIDTH = 512
RG_BLOCKS = 8
RG_BLOCK = MIX_WIDTH // RG_BLOCKS
RG_C = 8.0
CONV_WIDTH = 4
SB_HEADS = 8
SB_HEAD_DIM = MIX_WIDTH // SB_HEADS
Q_BLOCK = 128
HG_HEADS = 4
HG_KEY_DIM = MIX_WIDTH // HG_HEADS
HG_VAL_DIM = MIX_WIDTH // HG_HEADS
HG_CHUNK = 64
D_FF = 4 * D_MODEL
N_BRANCH = 3
N_NORMS = 4
EPS = 1e-6
LB_FLOOR = 1e-30
IN_WIDTHS = (MIX_WIDTH,) * 8 + (D_MODEL,) * 3
D_IN = 8 * MIX_WIDTH + 3 * D_MODEL

kernel_name = "hybrid_rglru_stickbreak_hgrn2_trunk"

def rms_norm(x, gain):
    xf = x.astype(jnp.float32)
    inv = lax.rsqrt(jnp.mean(xf * xf, axis=-1, keepdims=True) + EPS)
    return (xf * inv * gain.astype(jnp.float32)).astype(x.dtype)

def causal_depthwise_conv(x, w, b):
    S = x.shape[1]
    xp = jnp.pad(x, ((0, 0), (CONV_WIDTH - 1, 0), (0, 0)))
    out = sum(xp[:, k:k + S, :] * w[k] for k in range(CONV_WIDTH))
    return out + b

def rg_lru(x, w_a, b_a, w_x, b_x, lam):
    B, S, W = x.shape
    xf = x.astype(jnp.float32)
    xb = xf.reshape(B, S, RG_BLOCKS, RG_BLOCK)
    r = jax.nn.sigmoid(jnp.einsum('bsnc,ncd->bsnd', xb, w_a.astype(jnp.float32)).reshape(B, S, W) + b_a)
    i = jax.nn.sigmoid(jnp.einsum('bsnc,ncd->bsnd', xb, w_x.astype(jnp.float32)).reshape(B, S, W) + b_x)
    log_a = -RG_C * r * jax.nn.softplus(-lam.astype(jnp.float32))
    a = jnp.exp(log_a)
    mult = jnp.sqrt(jnp.maximum(-jnp.expm1(2.0 * log_a), 0.0))
    is_first = (jnp.arange(S) == 0)[None, :, None]
    mult = jnp.where(is_first, 1.0, mult)
    u = mult * (i * xf)

    def combine(e1, e2):
        a1, b1 = e1
        a2, b2 = e2
        return a1 * a2, a2 * b1 + b2

    _, h = lax.associative_scan(combine, (a, u), axis=1)
    return h.astype(x.dtype)

def stick_breaking_attention(q, k, v):
    B, S, H, Dh = q.shape
    n_blk = S // Q_BLOCK
    scale = Dh ** -0.5
    qb = q.astype(jnp.float32).reshape(B, n_blk, Q_BLOCK, H, Dh).transpose(1, 0, 3, 2, 4)
    kh = k.astype(jnp.float32).transpose(0, 2, 1, 3)
    vh = v.astype(jnp.float32).transpose(0, 2, 1, 3)
    s_pos = jnp.arange(S)
    starts = jnp.arange(n_blk) * Q_BLOCK

    def one_block(args):
        q_blk, start = args
        z = jnp.einsum('bhqd,bhsd->bhqs', q_blk, kh) * scale
        t_pos = start + jnp.arange(Q_BLOCK)
        causal = s_pos[None, :] < t_pos[:, None]
        log_keep = jnp.where(causal, jax.nn.log_sigmoid(-z), 0.0)
        suffix = lax.cumsum(log_keep, axis=3, reverse=True) - log_keep
        w = jnp.where(causal, jnp.exp(jax.nn.log_sigmoid(z) + suffix), 0.0)
        return jnp.einsum('bhqs,bhsd->bhqd', w, vh)

    out = lax.map(one_block, (qb, starts))
    out = out.transpose(1, 0, 3, 2, 4).reshape(B, S, H * Dh)
    return out.astype(q.dtype)

def hgrn2_recurrence(q, log_f, k, v):
    B, S, H, K = q.shape
    V = v.shape[-1]
    n = S // HG_CHUNK

    def to_chunks(t):
        return t.astype(jnp.float32).reshape(B, n, HG_CHUNK, H, t.shape[-1]).transpose(1, 0, 3, 2, 4)

    mask = jnp.tril(jnp.ones((HG_CHUNK, HG_CHUNK), dtype=bool))[:, :, None]

    def step(state, inp):
        qc, gc, kc, vc = inp
        b = jnp.cumsum(gc, axis=2)
        diff = b[:, :, :, None, :] - b[:, :, None, :, :]
        decay = jnp.where(mask, jnp.exp(jnp.where(mask, diff, 0.0)), 0.0)
        attn = jnp.einsum('bhtk,bhtsk,bhsk->bhts', qc, decay, kc)
        o = jnp.einsum('bhts,bhsv->bhtv', attn, vc) + jnp.einsum('bhtk,bhkv->bhtv', qc * jnp.exp(b), state)
        b_last = b[:, :, -1:, :]
        new_state = jnp.exp(b_last[:, :, 0, :])[..., None] * state + \
            jnp.einsum('bhsk,bhsv->bhkv', kc * jnp.exp(b_last - b), vc)
        return new_state, o

    init = jnp.zeros((B, H, K, V), jnp.float32)
    _, o = lax.scan(step, init, (to_chunks(q), to_chunks(log_f), to_chunks(k), to_chunks(v)))
    return o.transpose(1, 0, 3, 2, 4).reshape(B, S, H, V)

def hgrn2_branch(q_raw, f_raw, i_raw, g_raw, lb, norm_gain):
    B, S, _ = q_raw.shape
    shp = (B, S, HG_HEADS, HG_KEY_DIM)
    q = jax.nn.silu(q_raw.astype(jnp.float32)).reshape(shp)
    f_pre = f_raw.astype(jnp.float32).reshape(shp)
    lbh = lb.astype(jnp.float32).reshape(HG_HEADS, HG_KEY_DIM)
    log_f = jnp.logaddexp(jnp.log(jnp.maximum(lbh, LB_FLOOR)),
                          jnp.log1p(-lbh) + jax.nn.log_sigmoid(f_pre))
    k = (1.0 - lbh) * jax.nn.sigmoid(-f_pre)
    v = i_raw.astype(jnp.float32).reshape(B, S, HG_HEADS, HG_VAL_DIM)
    o = hgrn2_recurrence(q, log_f, k, v)
    o = o * lax.rsqrt(jnp.mean(o * o, axis=-1, keepdims=True) + EPS) * norm_gain.astype(jnp.float32)
    o = o.reshape(B, S, MIX_WIDTH) * jax.nn.silu(g_raw.astype(jnp.float32))
    return o.astype(q_raw.dtype)

def setup_inputs(seed: int = 0) -> dict:
    key = jax.random.key(seed)
    ks = jax.random.split(key, 20)
    f32 = jnp.float32
    nrm = lambda k, s: jax.random.normal(k, s, f32)
    x = nrm(ks[0], (BATCH, SEQ, D_MODEL))
    ln_gains = 1.0 + 0.02 * nrm(ks[1], (DEPTH, N_NORMS, D_MODEL))
    w_in = nrm(ks[2], (DEPTH, D_MODEL, D_IN)) * D_MODEL ** -0.5
    conv_w = nrm(ks[3], (DEPTH, CONV_WIDTH, MIX_WIDTH)) * CONV_WIDTH ** -0.5
    conv_b = 0.01 * nrm(ks[4], (DEPTH, MIX_WIDTH))
    rg_w_a = nrm(ks[5], (DEPTH, RG_BLOCKS, RG_BLOCK, RG_BLOCK)) * RG_BLOCK ** -0.5
    rg_b_a = 0.01 * nrm(ks[6], (DEPTH, MIX_WIDTH))
    rg_w_x = nrm(ks[7], (DEPTH, RG_BLOCKS, RG_BLOCK, RG_BLOCK)) * RG_BLOCK ** -0.5
    rg_b_x = 0.01 * nrm(ks[8], (DEPTH, MIX_WIDTH))
    u = jax.random.uniform(ks[9], (DEPTH, MIX_WIDTH), f32, minval=0.9, maxval=0.999)
    p = u ** (1.0 / RG_C)
    rg_lambda = jnp.log(p) - jnp.log1p(-p)
    lb_logits = 0.1 * nrm(ks[10], (DEPTH, MIX_WIDTH))
    hgrn_norm = 1.0 + 0.02 * nrm(ks[11], (DEPTH, HG_VAL_DIM))
    w_branch = nrm(ks[12], (DEPTH, N_BRANCH, MIX_WIDTH, D_MODEL)) * MIX_WIDTH ** -0.5
    w_out = nrm(ks[13], (DEPTH, D_MODEL, D_MODEL)) * D_MODEL ** -0.5
    w_up = nrm(ks[14], (DEPTH, D_MODEL, D_FF)) * D_MODEL ** -0.5
    w_down = nrm(ks[15], (DEPTH, D_FF, D_MODEL)) * D_FF ** -0.5
    return {"x": x, "ln_gains": ln_gains, "w_in": w_in, "conv_w": conv_w, "conv_b": conv_b,
            "rg_w_a": rg_w_a, "rg_b_a": rg_b_a, "rg_w_x": rg_w_x, "rg_b_x": rg_b_x,
            "rg_lambda": rg_lambda, "lb_logits": lb_logits, "hgrn_norm": hgrn_norm,
            "w_branch": w_branch, "w_out": w_out, "w_up": w_up, "w_down": w_down}

def reference(x, ln_gains, w_in, conv_w, conv_b, rg_w_a, rg_b_a, rg_w_x, rg_b_x,
              rg_lambda, lb_logits, hgrn_norm, w_branch, w_out, w_up, w_down):
    B, S, _ = x.shape
    split_points = [int(v) for v in np.cumsum(IN_WIDTHS)[:-1]]
    lb_p = jax.nn.softmax(lb_logits.astype(jnp.float32), axis=0)
    lower_bounds = jnp.cumsum(lb_p, axis=0) - lb_p[0:1]
    for l in range(DEPTH):
        h = rms_norm(x, ln_gains[l, 0])
        proj = h @ w_in[l]
        (rg_x, sb_q, sb_k, sb_v, hg_q, hg_f, hg_i, hg_g,
         gate_a, gate_b, gate_c) = jnp.split(proj, split_points, axis=-1)
        y_a = rg_lru(causal_depthwise_conv(rg_x, conv_w[l], conv_b[l]),
                     rg_w_a[l], rg_b_a[l], rg_w_x[l], rg_b_x[l], rg_lambda[l])
        hs = (B, S, SB_HEADS, SB_HEAD_DIM)
        y_b = stick_breaking_attention(sb_q.reshape(hs), sb_k.reshape(hs), sb_v.reshape(hs))
        y_c = hgrn2_branch(hg_q, hg_f, hg_i, hg_g, lower_bounds[l], hgrn_norm[l])
        merged = (jax.nn.sigmoid(gate_a) * (y_a @ w_branch[l, 0])
                  + jax.nn.sigmoid(gate_b) * (y_b @ w_branch[l, 1])
                  + jax.nn.sigmoid(gate_c) * (y_c @ w_branch[l, 2]))
        x = x + rms_norm(merged @ w_out[l], ln_gains[l, 1])
        h2 = rms_norm(x, ln_gains[l, 2])
        m = jnp.square(jax.nn.relu(h2 @ w_up[l])) @ w_down[l]
        x = x + rms_norm(m, ln_gains[l, 3])
    return x


_drawn_inputs = setup_inputs


def setup_inputs(seed=0):
    import zlib

    import numpy as np

    out = dict(_drawn_inputs(seed))
    spreads = {}
    factors = {}
    for name, (base, spread) in spreads.items():
        noise = np.random.default_rng([zlib.crc32(name.encode()), seed]).standard_normal(out[name].shape)
        drawn = base * np.exp(spread * noise) if base else spread * noise
        out[name] = __import__('jax').numpy.asarray(drawn.astype(out[name].dtype))
    for name, factor in factors.items():
        out[name] = (out[name] * factor).astype(out[name].dtype)
    return out
```

```python
from contextlib import ExitStack

import concourse.bass as bass
from concourse import mybir

F32 = mybir.dt.float32
F32R = mybir.dt.float32r
I8 = mybir.dt.int8
ALU = mybir.AluOpType
ACT = mybir.ActivationFunctionType

P = 128
RAW = 4
MRAW = 4
RING = 8
EPS = 1e-6
LB_FLOOR = 1e-30
RG_C = 8.0

GROUPS = [
    ("feat", 0),
    ("feat", 4), ("feat", 5), ("tok", 6),
    ("feat", 1), ("feat", 2), ("tok", 3),
    ("feat", 8), ("br", (0, 0)), ("feat", 9), ("br", (0, 1)),
    ("feat", 10), ("feat", 11), ("br", (1, 0)), ("br", (1, 1)),
    ("tok", 7),
    ("feat", 12), ("feat", 13), ("br", (2, 0)), ("br", (2, 1)),
    ("out", 0), ("out", 1),
]
G_RG, G_Q, G_F, G_I, G_SQ, G_SK, G_SV = range(7)
G_GA = (7, 9)
G_GB = (11, 12)
G_G = 15
G_GC = (16, 17)
G_OUT = (20, 21)
NS = 4 * len(GROUPS)
UNITS = [2 if kind == "br" else 4 for kind, _ in GROUPS]
FIRST_UNIT = [sum(UNITS[:g]) for g in range(len(GROUPS) + 1)]
NU = FIRST_UNIT[-1]
OWNER = [g for g, n in enumerate(UNITS) for _ in range(n)]
BY_ACT = {G_Q, G_I, G_SQ, G_SK, G_SV}

HG_AT = [12 + 4 * h for h in range(4)]
ATT_AT = [29 + 2 * a for a in range(8)]
ON_AT = 54
YC_AT = 64
LEVELS = (32, 16, 8, 4, 2, 1)


def split_slots():
    at = [[] for _ in range(NS)]
    for g in range(1, len(GROUPS)):
        for u in range(UNITS[g]):
            at[4 * (g - 1) + u * 4 // UNITS[g]].append(FIRST_UNIT[g] + u)
    for u in range(4):
        at[NS - 4 + u].append(NU + u)
    return at


def trunk(nc, x, ln_gains, w_in, conv_w, conv_b, rg_w_a, rg_b_a, rg_w_x, rg_b_x,
          rg_lambda, lb_logits, hgrn_norm, w_branch, w_out, w_up, w_down, out):
    _, S, D = x.shape
    W = conv_b.shape[1]
    FF = w_up.shape[2]
    assert (S, D, W, FF) == (512, 1024, 512, 4096)
    NF = FF // 1024
    SPLIT_AT = split_slots()

    win_v = w_in[0].rearrange("(u two p) (b n) -> b u p two n", two=2, p=P, n=512)
    wbr_v = w_branch[0].rearrange("b (u two p) (h n) -> b h u p two n", two=2, p=P, n=512)
    wout_v = w_out[0].rearrange("(u two p) (h n) -> h u p two n", two=2, p=P, n=512)
    wup_v = w_up[0].rearrange("(u two p) (i q n) -> i q u p two n", two=2, p=P, q=2, n=512)
    wdn_v = w_down[0].rearrange("(i u two p) (h n) -> i h u p two n", two=2, p=P, u=4, n=512)
    x_v = x[0].rearrange("(t p) d -> t p d", p=P)
    out_v = out[0].rearrange("(t p) d -> t p d", p=P)

    def unit_source(U):
        g = OWNER[U]
        u = U - FIRST_UNIT[g]
        kind, what = GROUPS[g]
        if kind == "br":
            return wbr_v[what[0], what[1], u]
        return wout_v[what, u] if kind == "out" else win_v[what, u]

    with ExitStack() as ctx:
        def sb(name, shape, dt=F32):
            return ctx.enter_context(nc.sbuf_tensor(name, shape, dt))

        def sem(name):
            return ctx.enter_context(nc.semaphore(name))

        whi = sb("whi", [P, RING, 2, 512], F32R)
        wlo = sb("wlo", [P, RING, 2, 512], F32R)
        hhi = sb("hhi", [P, 8, 512], F32R)
        hlo = sb("hlo", [P, 8, 512], F32R)
        yhi = sb("yhi", [P, 8, 512], F32R)
        ylo = sb("ylo", [P, 8, 512], F32R)
        raw = sb("raw", [P, RAW, 2, 512])
        arena = sb("arena", [P, 16896])

        def at(col, *dims):
            n = 1
            for d in dims:
                n *= d
            ap = arena[:, col:col + n]
            if len(dims) == 2:
                ap = ap.rearrange("p (a b) -> p a b", b=dims[1])
            return ap

        XPW = 515
        rg_xp = at(0, 4, XPW)
        rg_t = at(0, 4, 512)
        rg_xc = at(6160, 4, 512)
        rg_ri = at(8208, 8, 512)
        rg_a = at(12304, 4, 512)
        rg_wa = at(15872, 4, 128)
        rg_wx = at(16384, 4, 128)
        hg_b = at(0, 4, 512)
        hg_k = at(2048, 4, 512)
        hg_q = at(4096, 4, 512)
        hg_v = at(6144, 4, 512)
        lev_q = [at(12288, 512), at(12800, 512)]
        lev_k = [at(13312, 512), at(13824, 512)]
        attn_t = at(14336, 4, 128)
        qb = at(14848, 512)
        kdt = at(15360, 4, 128)
        states = at(15872, 7, 128)
        f0, f1, f2 = lev_q[0], lev_q[1], lev_k[0]
        sb_v = at(2048, 4, 512)
        sb_q = at(8192, 4, 512)
        sb_k = at(10240, 4, 512)
        stick = [at(12288, 1280), at(13568, 1280)]
        merged = [at(512 * j, 512) for j in range(4)] + [at(14848 + 512 * j, 512) for j in range(4)]
        gates = [at(4096, 4, 512), at(8192, 4, 512)]
        hg_g = at(10240, 4, 512)
        br_t = at(12288, 512)
        hg_sq = at(12800, 128)
        hgain = at(12928, 128)
        xin = at(0, 4, 1024)
        xn = [at(8192, 1024), at(9216, 1024)]
        xsq = at(10240, 1024)
        gain0 = at(11264, 1024)
        par_rows = at(12304, 128)
        x1 = at(0, 4, 1024)
        o4 = at(4096, 4, 1024)
        gain3 = at(8192, 1024)
        sq = at(9216, 1024)
        gain1 = at(10240, 1024)
        gain2 = at(11264, 1024)
        relu = [at(10240, 512), at(10752, 512)]
        hid = [at(11264, 512), at(11776, 512)]
        mraw = arena[:, 12288:16384].rearrange("p (u two n) -> p u two n", u=MRAW, two=2)

        ident = sb("ident", [P, P])
        ntri = sb("ntri", [P, P])
        nones = sb("nones", [P, P])
        masks = sb("masks", [P, len(LEVELS), P], I8)
        scan_keep = sb("scan_keep", [P, 512])
        NPAR = 36
        par = sb("par", [P, NPAR])
        c_conv = lambda k, j: par[:, 4 * k + j:4 * k + j + 1]
        c_convb, c_ba, c_bx, c_lam, c_lb = (par[:, 16 + 4 * i:20 + 4 * i] for i in range(5))
        chan = sb("chan", [P, 40])
        c8, c8n = chan[:, 0:4], chan[:, 4:8]
        ln1mlb, lnlb, ln_diff = chan[:, 8:12], chan[:, 12:16], chan[:, 16:20]
        ca, cb, cc = chan[:, 20:24], chan[:, 24:28], chan[:, 28:32]
        ss = sb("ss", [P, 4])
        rstd = sb("rstd", [P, 4])
        hg_ss = sb("hg_ss", [P, 16])
        hg_rstd = sb("hg_rstd", [P, 16])
        dec = sb("dec", [P, 8])
        epsb = sb("epsb", [P, 1])

        pmain = ctx.enter_context(nc.psum_tensor("pmain", [P, 2, 512], F32))
        pside = ctx.enter_context(nc.psum_tensor("pside", [P, 6, 512], F32))
        pz = pside[:, 0:3, :].rearrange("p a n -> p (a n)")
        pyb = pside[:, 3, :]
        ph = [pside[:, 4, :], pside[:, 5, :]]

        raw_in = [sem(f"raw_in{i}") for i in range(RAW)]
        mraw_in = [sem(f"mraw_in{i}") for i in range(MRAW)]
        x_in = [sem(f"x_in{i}") for i in range(4)]
        x_again = sem("x_again")
        par_in = sem("par_in")
        gain0_in = sem("gain0_in")
        rgw_in = sem("rgw_in")
        hgain_in = sem("hgain_in")
        gains_in = sem("gains_in")
        out_sent = sem("out_sent")
        w_hi, w_lo = sem("w_hi"), sem("w_lo")
        tile_done = sem("tile_done")
        act_free, dve_free = sem("act_free"), sem("dve_free")
        act_step, dve_step, pool_step = sem("act_step"), sem("dve_step"), sem("pool_step")
        const_ready = sem("const_ready")
        par_t = sem("par_t")
        par_ready = sem("par_ready")
        chan_a, chan_d = sem("chan_a"), sem("chan_d")
        rgw_zero = sem("rgw_zero")
        sq_done, rms_done = sem("sq_done"), sem("rms_done")
        mean_ready, n_sqrt = sem("mean_ready"), sem("n_sqrt")
        xn_ready, xn_t, h_hi, h_lo = sem("xn_ready"), sem("xn_t"), sem("h_hi"), sem("h_lo")
        rg_conv, rg_gate, rg_raw = sem("rg_conv"), sem("rg_gate"), sem("rg_raw")
        rg_act, rg_dve, ya_hi, ya_lo = sem("rg_act"), sem("rg_dve"), sem("ya_hi"), sem("ya_lo")
        q_ready = sem("q_ready")
        f_act, b_ready = sem("f_act"), sem("b_ready")
        lev_d, lev_e, lev_qe, lev_ke, lev_p, lev_m = (sem(f"lev_{n}") for n in ("d", "e", "qe", "ke", "p", "m"))
        kd_t, kd_ready, kv_done, st_ready, o_done, o_ready = (
            sem(n) for n in ("kd_t", "kd_ready", "kv_done", "st_ready", "o_done", "o_ready"))
        on_a, on_d, g_ready, oc_ready, oc_t, yc_hi, yc_lo = (
            sem(n) for n in ("on_a", "on_d", "g_ready", "oc_ready", "oc_t", "yc_hi", "yc_lo"))
        z_done, sp_ln, sp_ready, sp_masked, suf_done, w_exp, w_ready, av_done, yb_hi, yb_lo = (
            sem(n) for n in ("z_done", "sp_ln", "sp_ready", "sp_masked", "suf_done", "w_exp", "w_ready",
                             "av_done", "yb_hi", "yb_lo"))
        gate_ready, merged_sum, merged_hi, merged_lo = (
            sem(n) for n in ("gate_ready", "merged_sum", "merged_hi", "merged_lo"))
        relu_done, hid_done, hid_hi, hid_lo = (sem(n) for n in ("relu_done", "hid_done", "hid_hi", "hid_lo"))
        y_done = sem("y_done")

        block = ctx.enter_context(nc.Block())

        def free_count(s):
            mine = (s // 4) in BY_ACT
            n = sum(1 for r in range(s + 1) if ((r // 4) in BY_ACT) == mine)
            return (act_free if mine else dve_free), n

        DVE_FREE0 = sum(1 for r in range(NS) if (r // 4) not in BY_ACT)

        def hi_of(t):
            return t.bitcast(F32)

        @block.sync
        def _(sp):
            def load_unit(U):
                if U >= RAW:
                    sp.wait_ge(w_lo, U - RAW + 1)
                sp.dma_start(raw[:, U % RAW], unit_source(U)).then_inc(raw_in[U % RAW], 16)

            for t in range(4):
                sp.dma_start(xin[:, t], x_v[t]).then_inc(x_in[t], 16)
            sp.dma_start(gain0, ln_gains[0, 0:1, :].partition_broadcast(P)).then_inc(gain0_in, 16)
            sp.dma_start(par_rows[0:16], conv_w[0].rearrange("k (c p) -> (k c) p", p=P)).then_inc(par_in, 16)
            for i, v in enumerate((conv_b, rg_b_a, rg_b_x, rg_lambda, lb_logits)):
                sp.dma_start(par_rows[16 + 4 * i:20 + 4 * i],
                             v[0].rearrange("(c p) -> c p", p=P)).then_inc(par_in, 16)
            for U in range(RAW):
                load_unit(U)
            sp.wait_ge(rgw_zero, 1)
            for w, dst in ((rg_w_a, rg_wa), (rg_w_x, rg_wx)):
                for half in range(2):
                    src = w[0].rearrange("(j two) c d -> two c j d", two=2)[half]
                    sp.dma_start(dst[64 * half:64 * half + 64, :, 64 * half:64 * half + 64],
                                 src).then_inc(rgw_in, 16)
            for U in range(RAW, NU):
                if U == FIRST_UNIT[G_GB[1] + 1]:
                    sp.wait_ge(av_done, 8)
                    sp.dma_start(hgain, hgrn_norm[0:1, :].partition_broadcast(P)).then_inc(hgain_in, 16)
                load_unit(U)
            sp.wait_ge(merged_lo, 8)
            for t in range(4):
                sp.dma_start(x1[:, t], x_v[t]).then_inc(x_again, 16)
            for i, g in ((1, gain1), (2, gain2), (3, gain3)):
                sp.dma_start(g, ln_gains[0, i:i + 1, :].partition_broadcast(P)).then_inc(gains_in, 16)

            with sp.Fori(0, NF) as f:
                for g in range(4):
                    for u in range(4):
                        n = 4 * g + u
                        sp.wait_ge(w_lo, 16 * f + (NU + n - MRAW + 1))
                        src = wup_v[f, g, u] if g < 2 else wdn_v[f, g - 2, u]
                        sp.dma_start(mraw[:, n % MRAW], src).then_inc(mraw_in[n % MRAW], 16)
            for t in range(4):
                sp.wait_ge(y_done, t + 1)
                sp.dma_start(out_v[t], o4[:, t]).then_inc(out_sent, 16)
            sp.wait_ge(out_sent, 64)

        @block.gpsimd
        def _(pool):
            count = [0]

            def step(ins):
                count[0] += 1
                ins.then_inc(pool_step, 1)
                pool.wait_ge(pool_step, count[0])

            g = nc.gpsimd
            step(g.memset(ident[:], 0.0))
            step(g.affine_select(out=ident[:], in_=ident[:], compare_op=ALU.not_equal, fill=1.0, base=0,
                                 pattern=[[-1, P]], channel_multiplier=1))
            g.memset(epsb[:], EPS)
            g.memset(nones[:], -1.0)
            step(g.memset(ntri[:], -1.0))
            step(g.affine_select(out=ntri[:], in_=ntri[:], compare_op=ALU.is_ge, fill=0.0, base=0,
                                 pattern=[[-1, P]], channel_multiplier=1))
            step(g.memset(scan_keep[:], 1.0))
            g.memset(scan_keep[:].rearrange("p (c n) -> p c n", n=64)[:, :, 0:1], 0.0).then_inc(const_ready, 1)
            g.memset(rg_wa, 0.0)
            g.memset(rg_wx, 0.0).then_inc(rgw_zero, 1)
            step(g.memset(masks[:], 0))
            for l, m in enumerate(LEVELS):
                second = masks[:, l, :].rearrange("p (b two m) -> p b two m", two=2, m=m)[:, :, 1, :]
                nb = P // (2 * m)
                step(g.memset(second, 1))
                step(g.affine_select(out=second, in_=second, compare_op=ALU.is_ge, fill=0.0, base=0,
                                     pattern=[[-2 * m, nb], [0, m]], channel_multiplier=1))
                last = g.affine_select(out=second, in_=second, compare_op=ALU.is_ge, fill=0.0, base=m - 1,
                                       pattern=[[2 * m, nb], [0, m]], channel_multiplier=-1)
                if l < len(LEVELS) - 1:
                    step(last)
            last.then_inc(const_ready, 1)

            def level_k(h, p):
                if h == 0 and p == 0:
                    pool.wait_ge(f_act, 20)
                for i in range(2):
                    r = 2 * p + i
                    if r == 0:
                        continue
                    pool.wait_ge(lev_e, 7 * h + r)
                    if r >= 3:
                        pool.wait_ge(lev_p, 7 * h + r - 1)
                    elif h:
                        pool.wait_ge(lev_p, 7 * h)
                        pool.wait_ge(kd_t, h)
                    g.tensor_tensor(lev_k[i], hg_k[:, h], lev_q[i], ALU.mult).then_inc(lev_ke, 1)

            def causal(buf, done):
                diag = buf[:, 0:1152].rearrange("p (b n) -> p b n", n=128)[:, 0:9:4, :]
                g.affine_select(out=diag, in_=diag, compare_op=ALU.is_gt, fill=0.0, base=0,
                                pattern=[[0, 3], [1, P]], channel_multiplier=-1)
                g.affine_select(out=buf[:, 896:1024], in_=buf[:, 896:1024], compare_op=ALU.is_gt, fill=0.0,
                                base=0, pattern=[[1, P]], channel_multiplier=-1).then_inc(done, 1)

            for s in range(NS):
                for h, b in enumerate(HG_AT):
                    if b <= s < b + 4:
                        level_k(h, s - b)
                for a, b in enumerate(ATT_AT):
                    if s == b:
                        pool.wait_ge(sp_ready, a + 1)
                        causal(stick[a % 2], sp_masked)
                    if s == b + 1:
                        pool.wait_ge(w_exp, a + 1)
                        causal(stick[a % 2], w_ready)

        @block.scalar
        def _(act):
            a_ = nc.scalar
            n = {}

            def mark(ins, s):
                n[s.name] = n.get(s.name, 0) + 1
                ins.then_inc(s, 1)
                n["last"] = (s, n[s.name])

            def after():
                act.wait_ge(*n["last"])

            def step(ins):
                mark(ins, act_step)

            def split_hi(U):
                act.wait_ge(raw_in[U % RAW], 16 * (U // RAW + 1))
                if U >= RING:
                    act.wait_ge(tile_done, 4 * (OWNER[U - RING] + 1))
                mark(a_.activation(whi[:, U % RING], raw[:, U % RAW], ACT.Copy), w_hi)

            def split_hi_mlp(f, u):
                act.wait_ge(mraw_in[u % MRAW], 64 * f + 16 * (u // MRAW + 1))
                act.wait_ge(tile_done, 16 * f + (NS + 4 * (u // 4) - 4))
                a_.activation(whi[:, (NU + u) % RING], mraw[:, u % MRAW], ACT.Copy).then_inc(w_hi, 1)

            def mean_root(t):
                mark(a_.activation(ss[:, t:t + 1], ss[:, t:t + 1], ACT.Sqrt, bias=epsb[:], scale=1.0 / D), rms_done)

            act.wait_ge(const_ready, 2)
            for t in range(4):
                act.wait_ge(x_in[t], 16)
                step(a_.activation(xsq, xin[:, t], ACT.Square, accum_out=ss[:, t:t + 1]))
                after()
                mean_root(t)
            for t in range(4):
                act.wait_ge(xn_t, t + 1)
                src = pside[:, 2 * (t % 3):2 * (t % 3) + 2, :].rearrange("p a (b n) -> p (a b) n", n=P)
                mark(a_.activation(hhi[:, :, t * P:(t + 1) * P], src, ACT.Copy), h_hi)
            for U in range(4):
                split_hi(U)

            act.wait_ge(par_ready, 1)
            step(a_.activation(ca, c_lam, ACT.Abs))
            after()
            step(a_.activation(ca, ca, ACT.Exp, scale=-1.0))
            after()
            mark(a_.activation(ca, ca, ACT.Ln, bias=1.0), chan_a)
            act.wait_ge(chan_d, 2)
            mark(a_.activation(ln1mlb, cb, ACT.Ln, bias=1.0, scale=-1.0), chan_a)
            act.wait_ge(chan_d, 3)
            mark(a_.activation(lnlb, cc, ACT.Ln), chan_a)

            def forget_gate(h):
                ps = pmain[:, (4 * G_F + h) % 2]
                act.wait_ge(chan_d, 5)
                if h:
                    act.wait_ge(b_ready, h)
                else:
                    act.wait_ge(rg_dve, 8)
                step(a_.activation(f0, ps, ACT.Abs))
                after()
                step(a_.activation(f0, f0, ACT.Exp, scale=-1.0))
                after()
                mark(a_.activation(f0, f0, ACT.Ln, bias=1.0), f_act)
                act.wait_ge(*free_count(4 * G_F + h))
                mark(a_.activation(f0, f1, ACT.Abs, bias=ln_diff[:, h:h + 1]), f_act)
                after()
                mark(a_.activation(f0, f0, ACT.Exp, scale=-1.0), f_act)
                mark(a_.activation(hg_k[:, h], f2, ACT.Exp, scale=-1.0, bias=ln1mlb[:, h:h + 1]), f_act)
                after()
                mark(a_.activation(f0, f0, ACT.Ln, bias=1.0), f_act)

            def halves(buf, m):
                v = buf.rearrange("p (b two m) -> p b two m", two=2, m=m)
                return v[:, :, 0, :], v[:, :, 1, :]

            def level_exp(h, p):
                for i in range(2):
                    r = 2 * p + i
                    if r == 0:
                        continue
                    act.wait_ge(lev_d, 7 * h + r)
                    if r == 7:
                        mark(a_.activation(lev_q[i], lev_q[i], ACT.Exp, scale=-1.0), lev_e)
                    else:
                        first, second = halves(lev_q[i], LEVELS[r - 1])
                        a_.activation(first, first, ACT.Exp, scale=-1.0)
                        mark(a_.activation(second, second, ACT.Exp), lev_e)
                if p == 3:
                    if h:
                        act.wait_ge(o_done, h)
                        act.wait_ge(st_ready, 7 * h)
                    step(a_.activation(dec[:], hg_b[:, h].rearrange("p (c n) -> p c n", n=64)[:, :, 63], ACT.Exp))
                    mark(a_.activation(qb, hg_b[:, h], ACT.Exp), kd_ready)

            for s in range(NS):
                g, j = divmod(s, 4)
                for U in SPLIT_AT[s]:
                    if U < NU:
                        split_hi(U)
                    else:
                        split_hi_mlp(0, U - NU)
                for h, b in enumerate(HG_AT):
                    if b <= s < b + 4:
                        level_exp(h, s - b)
                ps = pmain[:, s % 2]
                if g in BY_ACT or g == G_F:
                    act.wait_ge(tile_done, s + 1)
                if g == G_Q:
                    mark(a_.activation(hg_q[:, j], ps, ACT.Copy), act_free)
                    if j == 3:
                        after()
                        mark(a_.activation(hg_q, hg_q, ACT.Silu), q_ready)
                if g == G_F:
                    forget_gate(j)
                if g == G_I:
                    if j == 0:
                        act.wait_ge(rg_dve, 8)
                    mark(a_.activation(hg_v[:, j], ps, ACT.Copy), act_free)
                if g == G_SQ:
                    act.wait_ge(ya_lo, 1)
                    mark(a_.activation(sb_q[:, j], ps, ACT.Copy, scale=0.125), act_free)
                if g == G_SK:
                    mark(a_.activation(sb_k[:, j], ps, ACT.Copy), act_free)
                if g == G_SV:
                    act.wait_ge(lev_ke, 7 * (j + 1))
                    act.wait_ge(lev_p, 7 * j + 1)
                    mark(a_.activation(sb_v[:, j], ps, ACT.Copy), act_free)

                if s == 6:
                    act.wait_ge(rg_raw, 8)
                    step(a_.activation(rg_ri, rg_ri, ACT.Sigmoid))
                    for j4 in range(4):
                        after()
                        mark(a_.activation(rg_a[:, j4], rg_ri[:, j4], ACT.Exp, scale=c8[:, j4:j4 + 1]), rg_act)
                    for j4 in range(4):
                        mark(a_.activation(rg_ri[:, j4], rg_ri[:, j4], ACT.Tanh, scale=c8n[:, j4:j4 + 1]), rg_act)
                if s == 7:
                    act.wait_ge(rg_dve, 2)
                    mark(a_.activation(rg_ri[:, 0:4], rg_ri[:, 0:4], ACT.Sqrt), rg_act)
                    act.wait_ge(rg_dve, 8)
                    mark(a_.activation(yhi[:, 0:4], rg_ri[:, 0:4], ACT.Copy), ya_hi)

                for h, b in enumerate(HG_AT):
                    if s == b + 3:
                        act.wait_ge(kd_t, h + 1)
                        if h:
                            act.wait_ge(kv_done, h)
                        mark(a_.activation(kdt, pside[:, 0, :].rearrange("p (a b) -> p a b", b=P), ACT.Copy), kd_ready)

                for a, b in enumerate(ATT_AT):
                    if s == b:
                        buf = stick[a % 2]
                        act.wait_ge(z_done, a + 1)
                        if a >= 2:
                            act.wait_ge(av_done, a - 1)
                        elif a == 0:
                            act.wait_ge(lev_p, 28)
                        else:
                            act.wait_ge(o_done, 4)
                        step(a_.activation(buf, pz[:, 0:1280], ACT.Abs))
                        after()
                        step(a_.activation(buf, buf, ACT.Exp, scale=-1.0))
                        after()
                        mark(a_.activation(buf, buf, ACT.Ln, bias=1.0), sp_ln)
                    if s == b + 1:
                        act.wait_ge(suf_done, a + 1)
                        mark(a_.activation(stick[a % 2], pz[:, 0:1280], ACT.Exp), w_exp)
                    if s == b + 2 and a % 2:
                        act.wait_ge(av_done, a + 1)
                        mark(a_.activation(yhi[:, 4 + a // 2], pyb, ACT.Copy), yb_hi)

                for k, gg in enumerate((*G_GA, *G_GB, *G_GC)):
                    if s == 4 * gg + 3:
                        act.wait_ge(dve_free, free_count(s)[1])
                        buf = gates[0 if k < 2 else k % 2]
                        mark(a_.activation(buf, buf, ACT.Sigmoid), gate_ready)
                if s == 4 * G_G + 3:
                    act.wait_ge(dve_free, free_count(s)[1])
                    mark(a_.activation(hg_g, hg_g, ACT.Silu), g_ready)

                if s == ON_AT:
                    act.wait_ge(o_ready, 4)
                    act.wait_ge(av_done, 8)
                    for i in range(16):
                        t, h = divmod(i, 4)
                        step(a_.activation(hg_sq, hg_v[:, t, h * P:(h + 1) * P], ACT.Square,
                                           accum_out=hg_ss[:, i:i + 1]))
                        after()
                    mark(a_.activation(hg_ss[:], hg_ss[:], ACT.Sqrt, bias=epsb[:], scale=1.0 / P), on_a)
                for t in range(4):
                    if s == YC_AT + t:
                        act.wait_ge(oc_t, t + 1)
                        mark(a_.activation(yhi[:, 0:4, t * P:(t + 1) * P],
                                           pside[:, t % 2].rearrange("p (a b) -> p a b", b=P), ACT.Copy), yc_hi)

                if GROUPS[g][0] == "br" and GROUPS[g][1][0] == 2:
                    d = 4 * GROUPS[g][1][1] + j
                    act.wait_ge(merged_sum, 8 + d + 1)
                    mark(a_.activation(hhi[:, d], merged[d], ACT.Copy), merged_hi)

                if g == G_OUT[1]:
                    act.wait_ge(dve_free, free_count(s)[1])
                    step(a_.activation(sq, o4[:, j], ACT.Square, accum_out=ss[:, j:j + 1]))
                    after()
                    mean_root(j)
                    act.wait_ge(mean_ready, 2 * j + 2)
                    step(a_.activation(sq, x1[:, j], ACT.Square, accum_out=ss[:, j:j + 1]))
                    after()
                    mean_root(j)

            def h2_round(t):
                act.wait_ge(xn_t, 4 + t + 1)
                src = pside[:, 2 * (t % 3):2 * (t % 3) + 2, :].rearrange("p a (b n) -> p (a b) n", n=P)
                mark(a_.activation(yhi[:, :, t * P:(t + 1) * P], src, ACT.Copy), h_hi)

            for t in range(4):
                h2_round(t)

            def mlp(f, last):
                for g in range(4):
                    for j in range(4):
                        k = 4 * g + j
                        if not (last and g == 3):
                            split_hi_mlp(f, k + 4)
                        if g < 2:
                            ps = pmain[:, (NS + k) % 2]
                            act.wait_ge(tile_done, 16 * f + (NS + k + 1))
                            if k >= 2:
                                act.wait_ge(hid_done, 8 * f + (k - 1))
                            a_.activation(relu[k % 2], ps, ACT.Relu).then_inc(relu_done, 1)
                            act.wait_ge(hid_done, 8 * f + (k + 1))
                            a_.activation(hhi[:, k], hid[k % 2], ACT.Copy).then_inc(hid_hi, 1)

            with act.Fori(0, NF - 1) as f:
                mlp(f, False)
            mlp(NF - 1, True)

            for t in range(4):
                act.wait_ge(dve_free, DVE_FREE0 + 8 * (NF - 1) + 4 + t + 1)
                step(a_.activation(sq, o4[:, t], ACT.Square, accum_out=ss[:, t:t + 1]))
                after()
                mean_root(t)

        @block.vector
        def _(dve):
            v = nc.vector
            n = {}

            def mark(ins, s):
                n[s.name] = n.get(s.name, 0) + 1
                ins.then_inc(s, 1)
                n["last"] = (s, n[s.name])

            def after():
                dve.wait_ge(*n["last"])

            def step(ins):
                mark(ins, dve_step)

            def split_lo(U):
                dve.wait_ge(w_hi, U + 1)
                mark(v.tensor_tensor(wlo[:, U % RING], raw[:, U % RAW], whi[:, U % RING].bitcast(F32), ALU.subtract), w_lo)

            def split_lo_mlp(f, u):
                dve.wait_ge(w_hi, 16 * f + (NU + u + 1))
                v.tensor_tensor(wlo[:, (NU + u) % RING], mraw[:, u % MRAW],
                                whi[:, (NU + u) % RING].bitcast(F32), ALU.subtract).then_inc(w_lo, 1)

            def take(dst, s):
                dve.wait_ge(tile_done, s + 1)
                mark(v.tensor_copy(dst, pmain[:, s % 2]), dve_free)

            def norm_scale(dst, src, t, gain, done):
                step(v.reciprocal(rstd[:, t:t + 1], ss[:, t:t + 1]))
                after()
                mark(v.scalar_tensor_tensor(dst, src, rstd[:, t:t + 1], gain, ALU.mult, ALU.mult), done)

            dve.wait_ge(gain0_in, 16)
            for t in range(4):
                dve.wait_ge(rms_done, t + 1)
                if t >= 2:
                    dve.wait_ge(xn_t, t - 1)
                norm_scale(xn[t % 2], xin[:, t], t, gain0, xn_ready)
            for t in range(4):
                src = pside[:, 2 * (t % 3):2 * (t % 3) + 2, :].rearrange("p a (b n) -> p (a b) n", n=P)
                dve.wait_ge(h_hi, t + 1)
                mark(v.tensor_tensor(hlo[:, :, t * P:(t + 1) * P], src,
                                     hhi[:, :, t * P:(t + 1) * P].bitcast(F32), ALU.subtract), h_lo)
            for U in range(4):
                split_lo(U)

            dve.wait_ge(par_t, 1)
            mark(v.tensor_copy(par[:], ph[0][:, 0:NPAR]), par_ready)
            after()
            dve.wait_ge(chan_a, 1)
            step(v.tensor_scalar(cb, c_lam, 0.0, None, ALU.min))
            after()
            step(v.tensor_tensor(ca, ca, cb, ALU.subtract))
            after()
            step(v.tensor_scalar(c8n, ca, RG_C, None, ALU.mult))
            mark(v.tensor_scalar(c8, ca, -RG_C, None, ALU.mult), chan_d)
            after()
            step(v.tensor_tensor(cb, c_lb, c_lb, ALU.subtract))
            after()
            step(v.tensor_scalar(cc, cb, 1.0, None, ALU.add))
            after()
            mark(v.tensor_tensor(cb, cc, cc, ALU.subtract), chan_d)
            after()
            mark(v.tensor_scalar(cc, cb, LB_FLOOR, 2.0 ** 50, ALU.max, ALU.mult), chan_d)
            dve.wait_ge(chan_a, 3)
            mark(v.tensor_scalar(lnlb, lnlb, -50.0 * 0.6931471805599453, None, ALU.add), chan_d)
            after()
            mark(v.tensor_tensor(ln_diff, ln1mlb, lnlb, ALU.subtract), chan_d)
            step(v.memset(rg_xp[:, :, 0:3], 0.0))
            after()

            def rg_bias(j):
                dve.wait_ge(rg_gate, j + 1)
                mark(v.tensor_scalar(rg_ri[:, j], ph[0], c_ba[:, j:j + 1], None, ALU.add), rg_raw)
                mark(v.tensor_scalar(rg_ri[:, 4 + j], ph[1], c_bx[:, j:j + 1], None, ALU.add), rg_raw)

            def forget_gate(h):
                ps = pmain[:, (4 * G_F + h) % 2]
                dve.wait_ge(f_act, 5 * h + 1)
                mark(v.scalar_tensor_tensor(f1, ps, 0.0, f0, ALU.min, ALU.subtract), dve_step)
                mark(v.scalar_tensor_tensor(f2, ps, 0.0, f0, ALU.max, ALU.add), dve_free)
                after()
                dve.wait_ge(f_act, 5 * h + 2)
                step(v.tensor_scalar(f1, f1, ln1mlb[:, h:h + 1], lnlb[:, h:h + 1], ALU.add, ALU.max))
                after()
                dve.wait_ge(f_act, 5 * h + 5)
                step(v.tensor_tensor(f1, f1, f0, ALU.add))
                after()
                mark(v.tensor_tensor_scan(hg_b[:, h], scan_keep[:], f1, 0.0, ALU.mult, ALU.add), b_ready)

            def level_prep(h, p):
                for i in range(2):
                    r = 2 * p + i
                    if r == 0:
                        continue
                    if 8 * h + r >= 2:
                        prev = 8 * h + r - 2
                        if prev % 8 == 7:
                            dve.wait_ge(lev_ke, 7 * (prev // 8 + 1))
                        elif prev % 8:
                            dve.wait_ge(lev_p, 7 * (prev // 8) + prev % 8 + 1)
                    if r == 7:
                        b64 = hg_b[:, h].rearrange("p (c n) -> p c n", n=64)
                        mark(v.tensor_tensor(lev_q[i].rearrange("p (c n) -> p c n", n=64), b64,
                                             b64[:, :, 63:64].to_broadcast((P, 8, 64)), ALU.subtract), lev_d)
                    else:
                        m = LEVELS[r - 1]
                        bb = hg_b[:, h].rearrange("p (c n) -> p c n", n=2 * m)
                        mark(v.tensor_tensor(lev_q[i].rearrange("p (c n) -> p c n", n=2 * m), bb,
                                             bb[:, :, m - 1:m].to_broadcast((P, S // (2 * m), 2 * m)),
                                             ALU.subtract), lev_d)
                for i in range(2):
                    r = 2 * p + i
                    if r in (0, 7):
                        continue
                    dve.wait_ge(lev_ke, 7 * h + r)
                    mark(v.tensor_tensor(lev_q[i], hg_q[:, h], lev_q[i], ALU.mult), lev_qe)
                if p == 3:
                    dve.wait_ge(kd_ready, 2 * h + 1)
                    mark(v.tensor_tensor(qb, hg_q[:, h], qb, ALU.mult), lev_qe)

            def level_merge(h, p):
                for i in range(2):
                    r = 2 * p + i
                    if r == 7:
                        continue
                    dve.wait_ge(lev_p, 7 * h + r + 1)
                    ps = ph[i].rearrange("p (a b) -> p a b", b=P)
                    if r == 0:
                        if h:
                            dve.wait_ge(kv_done, h)
                        mark(v.tensor_tensor(attn_t, ps, ident[:].unsqueeze(1).to_broadcast((P, 4, P)), ALU.mult), lev_m)
                    else:
                        after()
                        mark(v.copy_predicated(attn_t, masks[:, r - 1:r, :].to_broadcast((P, 4, P)), ps), lev_m)

            for s in range(NS):
                g, j = divmod(s, 4)
                for U in SPLIT_AT[s]:
                    split_lo(U) if U < NU else split_lo_mlp(0, U - NU)
                for h, b in enumerate(HG_AT):
                    if b <= s < b + 4:
                        if s == HG_AT[0]:
                            dve.wait_ge(q_ready, 1)
                            dve.wait_ge(b_ready, 4)
                        level_prep(h, s - b)

                ps = pmain[:, s % 2]
                if g == G_RG:
                    take(rg_xp[:, j, 3:XPW], s)
                    after()
                    step(v.tensor_scalar(rg_xc[:, j], rg_xp[:, j, 0:512], c_conv(0, j), c_convb[:, j:j + 1],
                                         ALU.mult, ALU.add))
                    for k in range(1, 4):
                        after()
                        ins = v.scalar_tensor_tensor(rg_xc[:, j], rg_xp[:, j, k:k + 512], c_conv(k, j), rg_xc[:, j],
                                                     ALU.mult, ALU.add)
                        mark(ins, rg_conv) if k == 3 else step(ins)
                if 2 <= s < 6:
                    rg_bias(s - 2)
                if s == 6:
                    dve.wait_ge(rg_act, 4)
                    mark(v.tensor_tensor(rg_t, rg_a, rg_a, ALU.mult), rg_dve)
                    after()
                    dve.wait_ge(rg_act, 8)
                    step(v.scalar_tensor_tensor(rg_ri[:, 0:4], rg_t, 1.0, rg_ri[:, 0:4], ALU.add, ALU.mult))
                    after()
                    mark(v.tensor_scalar(rg_ri[:, 0:4], rg_ri[:, 0:4], 0.0, None, ALU.max), rg_dve)
                    step(v.tensor_tensor(rg_t, rg_ri[:, 4:8], rg_xc, ALU.mult))
                    after()
                if s == 7:
                    dve.wait_ge(rg_act, 9)
                    mark(v.memset(rg_ri[:, 0:4, 0:1], 1.0), rg_dve)
                    after()
                    mark(v.tensor_tensor(rg_t, rg_t, rg_ri[:, 0:4], ALU.mult), rg_dve)
                    after()
                    for j4 in range(4):
                        mark(v.tensor_tensor_scan(rg_ri[:, j4], rg_a[:, j4], rg_t[:, j4], 0.0,
                                                  ALU.mult, ALU.add), rg_dve)
                    dve.wait_ge(ya_hi, 1)
                    mark(v.tensor_tensor(ylo[:, 0:4], rg_ri[:, 0:4], yhi[:, 0:4].bitcast(F32), ALU.subtract), ya_lo)
                if g == G_F:
                    dve.wait_ge(tile_done, s + 1)
                    forget_gate(j)

                for h, b in enumerate(HG_AT):
                    if b <= s < b + 4:
                        level_merge(h, s - b)
                    if s == b + 4:
                        dve.wait_ge(kv_done, h + 1)
                        if h:
                            dve.wait_ge(o_done, h)
                        for c in range(7):
                            kv = pside[:, 1 + c % 2, (c // 2) * P:(c // 2 + 1) * P]
                            if c == 0:
                                mark(v.tensor_copy(states[:, 0], kv), st_ready)
                            else:
                                after()
                                mark(v.scalar_tensor_tensor(states[:, c], states[:, c - 1], dec[:, c:c + 1], kv,
                                                            ALU.mult, ALU.add), st_ready)
                    if s == b + 5:
                        dve.wait_ge(o_done, h + 1)
                        mark(v.tensor_copy(hg_v[:, :, h * P:(h + 1) * P], pyb.rearrange("p (a b) -> p a b", b=P)), o_ready)

                for k, gg in enumerate((*G_GA, *G_GB, *G_GC)):
                    if g == gg:
                        if gg == G_GB[1] and j == 0:
                            dve.wait_ge(z_done, 8)
                        if gg == G_GA[0] and j == 0:
                            dve.wait_ge(lev_p, 28)
                        take(gates[0 if k < 2 else k % 2][:, j], s)
                if g == G_G:
                    if j == 0:
                        dve.wait_ge(z_done, 8)
                    take(hg_g[:, j], s)

                for a, b in enumerate(ATT_AT):
                    if s == b:
                        dve.wait_ge(sp_ln, a + 1)
                        mark(v.scalar_tensor_tensor(stick[a % 2], pz[:, 0:1280], 0.0, stick[a % 2],
                                                    ALU.max, ALU.add), sp_ready)
                    if s == b + 2 and a % 2:
                        dve.wait_ge(yb_hi, a // 2 + 1)
                        mark(v.tensor_tensor(ylo[:, 4 + a // 2], pyb, yhi[:, 4 + a // 2].bitcast(F32), ALU.subtract), yb_lo)

                if GROUPS[g][0] == "br":
                    branch, half = GROUPS[g][1]
                    d = 4 * half + j
                    dve.wait_ge(gate_ready, 2 * branch + half + 1)
                    gate = gates[half if branch else 0][:, j]
                    dve.wait_ge(tile_done, s + 1)
                    if branch == 0:
                        mark(v.tensor_tensor(merged[d], ps, gate, ALU.mult), dve_free)
                    else:
                        mark(v.tensor_tensor(br_t, ps, gate, ALU.mult), dve_free)
                        after()
                        mark(v.tensor_tensor(merged[d], merged[d], br_t, ALU.add), merged_sum)
                        after()
                    if branch == 2:
                        dve.wait_ge(merged_hi, d + 1)
                        mark(v.tensor_tensor(hlo[:, d], merged[d], hhi[:, d].bitcast(F32), ALU.subtract), merged_lo)

                if s == ON_AT + 1:
                    dve.wait_ge(on_a, 1)
                    dve.wait_ge(hgain_in, 16)
                    step(v.reciprocal(hg_rstd[:], hg_ss[:]))
                    after()
                    for i in range(16):
                        t, h = divmod(i, 4)
                        o = hg_v[:, t, h * P:(h + 1) * P]
                        mark(v.scalar_tensor_tensor(o, o, hg_rstd[:, i:i + 1], hgain, ALU.mult, ALU.mult), on_d)
                if s == 4 * G_G + 3:
                    dve.wait_ge(g_ready, 1)
                    for t in range(4):
                        mark(v.tensor_tensor(hg_v[:, t], hg_v[:, t], hg_g[:, t], ALU.mult), oc_ready)
                for t in range(4):
                    if s == YC_AT + t:
                        dve.wait_ge(yc_hi, t + 1)
                        mark(v.tensor_tensor(ylo[:, 0:4, t * P:(t + 1) * P],
                                             pside[:, t % 2].rearrange("p (a b) -> p a b", b=P),
                                             yhi[:, 0:4, t * P:(t + 1) * P].bitcast(F32), ALU.subtract), yc_lo)

                if g in G_OUT:
                    take(o4[:, j, 512 * (g - G_OUT[0]):512 * (g - G_OUT[0]) + 512], s)
                if g == G_OUT[1]:
                    if j == 0:
                        dve.wait_ge(gains_in, 48)
                        dve.wait_ge(x_again, 64)
                    dve.wait_ge(rms_done, 4 + 2 * j + 1)
                    norm_scale(o4[:, j], o4[:, j], j, gain1, mean_ready)
                    after()
                    mark(v.tensor_tensor(x1[:, j], x1[:, j], o4[:, j], ALU.add), mean_ready)
                    dve.wait_ge(rms_done, 4 + 2 * j + 2)
                    norm_scale(o4[:, j], x1[:, j], j, gain2, xn_ready)

            for t in range(4):
                src = pside[:, 2 * (t % 3):2 * (t % 3) + 2, :].rearrange("p a (b n) -> p (a b) n", n=P)
                dve.wait_ge(h_hi, 4 + t + 1)
                mark(v.tensor_tensor(ylo[:, :, t * P:(t + 1) * P], src,
                                     yhi[:, :, t * P:(t + 1) * P].bitcast(F32), ALU.subtract), h_lo)
            step(v.memset(o4, 0.0))
            after()

            def mlp(f, last):
                for g in range(4):
                    for j in range(4):
                        k = 4 * g + j
                        if not (last and g == 3):
                            split_lo_mlp(f, k + 4)
                        ps = pmain[:, (NS + k) % 2]
                        if g < 2:
                            dve.wait_ge(relu_done, 8 * f + (k + 1))
                            if k >= 2:
                                dve.wait_ge(hid_lo, 8 * f + (k - 1))
                            v.scalar_tensor_tensor(hid[k % 2], ps, 0.0, relu[k % 2], ALU.max, ALU.mult).then_inc(hid_done, 1)
                            dve.wait_ge(hid_hi, 8 * f + (k + 1))
                            v.tensor_tensor(hlo[:, k], hid[k % 2], hhi[:, k].bitcast(F32), ALU.subtract).then_inc(hid_lo, 1)
                        else:
                            part = o4[:, j, 512 * (g - 2):512 * (g - 2) + 512]
                            dve.wait_ge(tile_done, 16 * f + (NS + k + 1))
                            v.tensor_tensor(part, part, ps, ALU.add).then_inc(dve_free, 1)

            with dve.Fori(0, NF - 1) as f:
                mlp(f, False)
            mlp(NF - 1, True)

            for t in range(4):
                dve.wait_ge(rms_done, 12 + t + 1)
                step(v.reciprocal(rstd[:, t:t + 1], ss[:, t:t + 1]))
                after()
                step(v.scalar_tensor_tensor(o4[:, t], o4[:, t], rstd[:, t:t + 1], gain3, ALU.mult, ALU.mult))
                after()
                mark(v.tensor_tensor(o4[:, t], o4[:, t], x1[:, t], ALU.add), y_done)

        @block.tensor
        def _(pe):
            mm = nc.tensor.matmul

            def product(dst, left, right, k, last_k):
                mm(dst, left[0], right[0], start=(k == 0), stop=False)
                mm(dst, left[0], right[1], start=False, stop=False)
                return mm(dst, left[1], right[0], start=False, stop=(k == last_k))

            def ring(U0, k):
                U = (U0 + k // 2) % RING
                return whi[:, U, k % 2], wlo[:, U, k % 2]

            def transposes(src, t, dst_bank, nk):
                for k in range(nk):
                    last = nc.tensor.transpose(pside[:, dst_bank + k // 4, (k % 4) * P:(k % 4 + 1) * P],
                                               src[:, k * P:(k + 1) * P], ident[:])
                return last

            pe.wait_ge(const_ready, 1)
            for t in range(4):
                pe.wait_ge(xn_ready, t + 1)
                if t == 3:
                    pe.wait_ge(h_lo, 1)
                transposes(xn[t % 2], t, 2 * (t % 3), 8).then_inc(xn_t, 1)
            pe.wait_ge(par_in, 96)
            pe.wait_ge(h_lo, 3)
            nc.tensor.transpose(ph[0][:, 0:NPAR], par_rows[0:NPAR, :], ident[0:NPAR, 0:NPAR]).then_inc(par_t, 1)
            pe.wait_ge(h_lo, 4)

            def main(s):
                g, j = divmod(s, 4)
                kind = GROUPS[g][0]
                if s >= 2:
                    pe.wait_ge(*free_count(s - 2))
                dst = pmain[:, s % 2]
                nk = 4 if kind == "br" else 8
                y0 = 0 if kind != "br" else (0, 4, 0)[GROUPS[g][1][0]]
                for k in range(nk):
                    if j == 0 and k % 2 == 0:
                        pe.wait_ge(w_lo, FIRST_UNIT[g] + k // 2 + 1)
                    if kind == "out" and s == 4 * G_OUT[0]:
                        pe.wait_ge(merged_lo, k + 1)
                    w = ring(FIRST_UNIT[g], k)
                    if kind in ("feat", "br"):
                        left = tuple(x[:, j * P:(j + 1) * P] for x in w)
                        right = (hhi[:, k], hlo[:, k]) if kind == "feat" else (yhi[:, y0 + k], ylo[:, y0 + k])
                    else:
                        left = (hhi[:, k, j * P:(j + 1) * P], hlo[:, k, j * P:(j + 1) * P])
                        right = w
                    last = product(dst, left, right, k, nk - 1)
                last.then_inc(tile_done, 1)

            def rg_gates(j):
                pe.wait_ge(rg_conv, j + 1)
                if j == 0:
                    pe.wait_ge(rgw_in, 64)
                    pe.wait_ge(par_ready, 1)
                else:
                    pe.wait_ge(rg_raw, 2 * j)
                mm(ph[0], rg_wa[:, j], rg_xc[:, j], start=True, stop=True)
                mm(ph[1], rg_wx[:, j], rg_xc[:, j], start=True, stop=True).then_inc(rg_gate, 1)

            def levels(h, p):
                for i in range(2):
                    r = 2 * p + i
                    if r == 7:
                        pe.wait_ge(lev_ke, 7 * h + 7)
                        if h:
                            pe.wait_ge(kd_ready, 2 * h)
                        transposes(lev_k[1], 0, 0, 4).then_inc(kd_t, 1)
                        continue
                    if r == 0:
                        pe.wait_ge(b_ready, h + 1)
                        pe.wait_ge(q_ready, 1)
                        kk, qq = hg_k[:, h], hg_q[:, h]
                    else:
                        pe.wait_ge(lev_ke, 7 * h + r)
                        pe.wait_ge(lev_qe, 7 * h + r)
                        kk, qq = lev_k[i], lev_q[i]
                    if h == 0 and r < 2:
                        pe.wait_ge(rg_raw, 8)
                    else:
                        pe.wait_ge(lev_m, 7 * h + max(r - 1, 0))
                    for t in range(4):
                        c = slice(t * P, (t + 1) * P)
                        last = mm(ph[i][:, c], kk[:, c], qq[:, c], start=True, stop=True)
                    last.then_inc(lev_p, 1)

            def chunk_products(h):
                pe.wait_ge(lev_m, 7 * (h + 1))
                pe.wait_ge(kd_ready, 2 * h + 2)
                if h:
                    pe.wait_ge(o_ready, h)
                    pe.wait_ge(st_ready, 7 * h)
                else:
                    pe.wait_ge(act_free, free_count(4 * G_I + 3)[1])
                for t in range(4):
                    mm(pyb[:, t * P:(t + 1) * P], attn_t[:, t], hg_v[:, t, h * P:(h + 1) * P],
                       start=(t == 0), stop=False, skip_group_check=True)
                for c in range(7):
                    rows = slice(64 * (c % 2), 64 * (c % 2) + 64)
                    last = mm(pside[:, 1 + c % 2, (c // 2) * P:(c // 2 + 1) * P], kdt[rows, c // 2],
                              hg_v[rows, c // 2, h * P:(h + 1) * P], start=True, stop=True)
                last.then_inc(kv_done, 1)

            def state_products(h):
                pe.wait_ge(st_ready, 7 * (h + 1))
                pe.wait_ge(lev_qe, 7 * (h + 1))
                for c in range(1, 8):
                    rows = slice(64 * (c % 2), 64 * (c % 2) + 64)
                    last = mm(pyb[rows, (c // 2) * P:(c // 2 + 1) * P], qb[:, 64 * c:64 * c + 64],
                              states[:, c - 1], start=False, stop=(c == 7), skip_group_check=True)
                last.then_inc(o_done, 1)

            Z_AT = (0, 512, 1024, 896)

            def att_z(a):
                rows = slice(64 * (a % 2), 64 * (a % 2) + 64)
                if a == 0:
                    pe.wait_ge(act_free, free_count(4 * G_SV + 3)[1])
                    pe.wait_ge(st_ready, 28)
                    pe.wait_ge(kd_ready, 8)
                else:
                    pe.wait_ge(w_exp, a)
                for b in (0, 1, 3, 2):
                    last = mm(pz[:, Z_AT[b]:Z_AT[b] + S - P * b], sb_k[rows, a // 2, b * P:(b + 1) * P],
                              sb_q[rows, a // 2, b * P:S], start=(b != 3), stop=False, skip_group_check=True)
                last.then_inc(z_done, 1)

            def att_suffix(a):
                pe.wait_ge(sp_masked, a + 1)
                sp_ = stick[a % 2]
                for b in range(4):
                    for c in range(b, 4):
                        last = mm(pz[:, Z_AT[b] + P * (c - b):Z_AT[b] + S - P * b],
                                  ntri[:] if c == b else nones[:], sp_[:, Z_AT[c]:Z_AT[c] + S - P * c],
                                  start=False, stop=(c == 3), skip_group_check=True)
                last.then_inc(suf_done, 1)

            def att_out(a):
                pe.wait_ge(w_ready, a + 1)
                if a == 0:
                    pe.wait_ge(o_ready, 4)
                elif a % 2 == 0:
                    pe.wait_ge(yb_lo, a // 2)
                rows = slice(64 * (a % 2), 64 * (a % 2) + 64)
                for b in range(4):
                    last = mm(pyb[rows, b * P:S], sb_v[:, b, 64 * a:64 * a + 64],
                              stick[a % 2][:, Z_AT[b]:Z_AT[b] + S - P * b],
                              start=(b == 0), stop=(b == 3), skip_group_check=True)
                last.then_inc(av_done, 1)

            for s in range(NS):
                if s == 4 * 8:
                    pe.wait_ge(ya_lo, 1)
                if s == 4 * 13:
                    pe.wait_ge(yb_lo, 4)
                if s == 4 * 18:
                    pe.wait_ge(yc_lo, 4)
                main(s)
                if 2 <= s < 6:
                    rg_gates(s - 2)
                for h, b in enumerate(HG_AT):
                    if s == b + 4:
                        chunk_products(h)
                for h, b in enumerate(HG_AT):
                    if b <= s < b + 4:
                        levels(h, s - b)
                    if s == b + 5:
                        state_products(h)
                for a, b in enumerate(ATT_AT):
                    if s == b + 2:
                        att_out(a)
                for a, b in enumerate(ATT_AT):
                    if s == b:
                        att_z(a)
                    if s == b + 1:
                        att_suffix(a)
                for t in range(4):
                    if s == YC_AT + t:
                        pe.wait_ge(oc_ready, t + 1)
                        if t >= 2:
                            pe.wait_ge(yc_lo, t - 1)
                        transposes(hg_v[:, t], t, t % 2, 4).then_inc(oc_t, 1)
            for t in range(4):
                pe.wait_ge(xn_ready, 4 + t + 1)
                if t == 3:
                    pe.wait_ge(h_lo, 5)
                transposes(o4[:, t], t, 2 * (t % 3), 8).then_inc(xn_t, 1)
            pe.wait_ge(h_lo, 8)

            def mlp(f):
                for g in range(4):
                    for j in range(4):
                        k = 4 * g + j
                        if k in (0, 1):
                            pe.wait_ge(dve_free, 8 * f + (DVE_FREE0 - 1 + k))
                        elif k < 10:
                            pe.wait_ge(hid_done, 8 * f + (k - 1))
                        else:
                            pe.wait_ge(dve_free, 8 * f + (DVE_FREE0 + k - 9))
                        dst = pmain[:, (NS + k) % 2]
                        for kt in range(8):
                            if j == 0 and kt % 2 == 0:
                                pe.wait_ge(w_lo, 16 * f + (NU + 4 * g + kt // 2 + 1))
                            if k == 8:
                                pe.wait_ge(hid_lo, 8 * f + (kt + 1))
                            w = ring(NU + 4 * g, kt)
                            if g < 2:
                                last = product(dst, tuple(x[:, j * P:(j + 1) * P] for x in w),
                                               (yhi[:, kt], ylo[:, kt]), kt, 7)
                            else:
                                last = product(dst, (hhi[:, kt, j * P:(j + 1) * P], hlo[:, kt, j * P:(j + 1) * P]),
                                               w, kt, 7)
                        last.then_inc(tile_done, 1)

            with pe.Fori(0, NF) as f:
                mlp(f)


_INS = ["x", "ln_gains", "w_in", "conv_w", "conv_b", "rg_w_a", "rg_b_a", "rg_w_x", "rg_b_x", "rg_lambda",
        "lb_logits", "hgrn_norm", "w_branch", "w_out", "w_up", "w_down"]


def kernel(**inputs):
    import numpy as _np
    import concourse.bacc as _bacc
    from concourse import mybir as _mybir
    from concourse.bass_utils import run_bass_kernel_spmd as _run

    nc = _bacc.Bacc("TRN2", target_bir_lowering=False, num_devices=1, dynamic_dma_scratch_size=1024)
    arrays, args = {}, []
    for name in _INS:
        a = _np.ascontiguousarray(inputs[name])
        arrays[f"in_{name}"] = a
        args.append(nc.dram_tensor(f"in_{name}", a.shape, _mybir.dt.from_np(a.dtype), kind="ExternalInput").ap())
    shape = inputs["x"].shape
    args.append(nc.dram_tensor("out_x", shape, _mybir.dt.float32, kind="ExternalOutput").ap())
    trunk(nc, *args)
    r = _run(nc, [arrays], core_ids=[0])
    return r.results[0]["out_x"]
```

```python
from contextlib import ExitStack

import concourse.bass as bass
from concourse import mybir

F32 = mybir.dt.float32
F32R = mybir.dt.float32r
I8 = mybir.dt.int8
ALU = mybir.AluOpType
ACT = mybir.ActivationFunctionType

P = 128
RAW = 4
MRAW = 4
RING = 8
EPS = 1e-6
LB_FLOOR = 1e-30
RG_C = 8.0
EXP_SET = "exp_and_others"
EXP_LN_SET = "natural_log_exp_and_others"
SIGMOID_SET = "sigmoid_and_others"
SILU_SET = "silu_and_others"
SQRT_SET = "sqrt_and_others"

GROUPS = [
    ("tok", 6),
    ("feat", 0),
    ("feat", 4), ("feat", 5),
    ("feat", 1), ("feat", 2), ("tok", 3),
    ("feat", 8), ("br", (0, 0)), ("feat", 9), ("br", (0, 1)),
    ("feat", 10), ("feat", 11), ("br", (1, 0)), ("br", (1, 1)),
    ("tok", 7),
    ("feat", 12), ("feat", 13), ("br", (2, 0)), ("br", (2, 1)),
    ("out", 0), ("out", 1),
]
G_I, G_RG, G_Q, G_F, G_SQ, G_SK, G_SV = range(7)
G_GA = (7, 9)
G_GB = (11, 12)
G_G = 15
G_GC = (16, 17)
G_OUT = (20, 21)
RG_AT = 4 * G_RG
NS = 4 * len(GROUPS)
UNITS = [2 if kind == "br" else 4 for kind, _ in GROUPS]
FIRST_UNIT = [sum(UNITS[:g]) for g in range(len(GROUPS) + 1)]
NU = FIRST_UNIT[-1]
OWNER = [g for g, n in enumerate(UNITS) for _ in range(n)]
BY_ACT = {G_Q, G_I, G_SQ, G_SK, G_SV, *G_OUT}

HG_AT = [16 + 4 * h for h in range(4)]
ATT_AT = [33 + 2 * a for a in range(8)]
ON_AT = 54
YC_AT = 64
LEVELS = (32, 16, 8, 4, 2, 1)


def split_slots():
    at = [[] for _ in range(NS)]
    for g in range(1, len(GROUPS)):
        for u in range(UNITS[g]):
            at[4 * (g - 1) + u * 4 // UNITS[g]].append(FIRST_UNIT[g] + u)
    for u in range(4):
        at[NS - 4 + u].append(NU + u)
    return at


def trunk(nc, x, ln_gains, w_in, conv_w, conv_b, rg_w_a, rg_b_a, rg_w_x, rg_b_x,
          rg_lambda, lb_logits, hgrn_norm, w_branch, w_out, w_up, w_down, out):
    _, S, D = x.shape
    W = conv_b.shape[1]
    FF = w_up.shape[2]
    assert (S, D, W, FF) == (512, 1024, 512, 4096)
    NF = FF // 1024
    SPLIT_AT = split_slots()

    win_v = w_in[0].rearrange("(u two p) (b n) -> b u p two n", two=2, p=P, n=512)
    wbr_v = w_branch[0].rearrange("b (u two p) (h n) -> b h u p two n", two=2, p=P, n=512)
    wout_v = w_out[0].rearrange("(u two p) (h n) -> h u p two n", two=2, p=P, n=512)
    wup_v = w_up[0].rearrange("(u two p) (i q n) -> i q u p two n", two=2, p=P, q=2, n=512)
    wdn_v = w_down[0].rearrange("(i u two p) (h n) -> i h u p two n", two=2, p=P, u=4, n=512)
    x_v = x[0].rearrange("(t p) d -> t p d", p=P)
    out_v = out[0].rearrange("(t p) d -> t p d", p=P)

    def unit_source(U):
        g = OWNER[U]
        u = U - FIRST_UNIT[g]
        kind, what = GROUPS[g]
        if kind == "br":
            return wbr_v[what[0], what[1], u]
        return wout_v[what, u] if kind == "out" else win_v[what, u]

    with ExitStack() as ctx:
        def sb(name, shape, dt=F32):
            return ctx.enter_context(nc.sbuf_tensor(name, shape, dt))

        def sem(name):
            return ctx.enter_context(nc.semaphore(name))

        whi = sb("whi", [P, RING, 2, 512], F32R)
        wlo = sb("wlo", [P, RING, 2, 512], F32R)
        hhi = sb("hhi", [P, 8, 512], F32R)
        hlo = sb("hlo", [P, 8, 512], F32R)
        yhi = sb("yhi", [P, 8, 512], F32R)
        ylo = sb("ylo", [P, 8, 512], F32R)
        raw = sb("raw", [P, RAW, 2, 512])
        arena = sb("arena", [P, 18944])

        def at(col, *dims):
            n = 1
            for d in dims:
                n *= d
            ap = arena[:, col:col + n]
            if len(dims) == 2:
                ap = ap.rearrange("p (a b) -> p a b", b=dims[1])
            return ap

        XPW = 515
        rg_xp = at(0, 4, XPW)
        rg_t = at(0, 4, 512)
        rg_xc = at(14336, 4, 512)
        rg_ri = at(8192, 8, 512)
        rg_a = at(12288, 4, 512)
        rg_wa = at(16384, 4, 128)
        rg_wx = at(5632, 4, 128)
        hg_b = at(0, 4, 512)
        hg_k = at(2048, 4, 512)
        hg_q = at(4096, 4, 512)
        hg_v = at(6144, 4, 512)
        lev_q = [at(12288, 512), at(12800, 512)]
        lev_k = [at(13312, 512), at(13824, 512)]
        attn_t = at(14336, 4, 128)
        qb = at(14848, 512)
        kdt = at(15360, 4, 128)
        states = at(15872, 7, 128)
        f0, f1, f2 = lev_q[0], lev_q[1], lev_k[0]
        sb_v = at(16896, 4, 512)
        sb_q = at(8192, 4, 512)
        sb_k = at(10240, 4, 512)
        stick = [at(12288, 1280), at(13568, 1280)]
        merged = [at(512 * j, 512) for j in range(4)] + [at(14848 + 512 * j, 512) for j in range(4)]
        gates = [at(2048, 4, 512), at(4096, 4, 512), at(4096, 4, 512), at(8192, 4, 512),
                 at(4096, 4, 512), at(8192, 4, 512)]
        hg_g = at(10240, 4, 512)
        br_t = [at(12288, 512), at(13056, 512)]
        hg_sq = at(12800, 128)
        hgain = at(12928, 128)
        xin = at(0, 4, 1024)
        xn = [at(8192, 1024), at(9216, 1024)]
        xsq = at(10240, 1024)
        gain0 = at(11264, 1024)[0:1]
        par_rows = at(12288, 128)
        ones_row = at(12544, P)[0:1]
        x1 = at(0, 4, 1024)
        o4 = at(4096, 4, 1024)
        gain3 = at(8192, 1024)
        sq = at(9216, 1024)
        gain1 = at(10240, 1024)
        gain2 = at(11264, 1024)
        relu = [at(10240, 512), at(10752, 512)]
        hid = [at(11264, 512), at(11776, 512)]
        mraw = arena[:, 12288:16384].rearrange("p (u two n) -> p u two n", u=MRAW, two=2)

        ident = sb("ident", [P, P])
        ntri = sb("ntri", [P, P])
        nones = sb("nones", [P, P])
        masks = sb("masks", [P, len(LEVELS), P], I8)
        scan_keep = sb("scan_keep", [P, 512])
        NPAR = 36
        par = sb("par", [P, NPAR])
        c_conv = lambda k, j: par[:, 4 * k + j:4 * k + j + 1]
        c_convb, c_ba, c_bx, c_lam, c_lb = (par[:, 16 + 4 * i:20 + 4 * i] for i in range(5))
        chan = sb("chan", [P, 40])
        c8, c8n = chan[:, 0:4], chan[:, 4:8]
        ln1mlb, lnlb, ln_diff = chan[:, 8:12], chan[:, 12:16], chan[:, 16:20]
        ca, cb, cc = chan[:, 20:24], chan[:, 24:28], chan[:, 28:32]
        ss = sb("ss", [P, 4])
        ss_half, ms_half = chan[:, 32:36], chan[:, 36:40]
        rstd = sb("rstd", [P, 4])
        hg_ss = sb("hg_ss", [P, 16])
        hg_rstd = sb("hg_rstd", [P, 16])
        dec = sb("dec", [P, 8])
        epsb = sb("epsb", [P, 1])

        pmain = ctx.enter_context(nc.psum_tensor("pmain", [P, 2, 512], F32))
        pside = ctx.enter_context(nc.psum_tensor("pside", [P, 6, 512], F32))
        pz = pside[:, 0:3, :].rearrange("p a n -> p (a n)")
        pyb = pside[:, 3, :]
        ph = [pside[:, 4, :], pside[:, 5, :]]

        raw_in = [sem(f"raw_in{i}") for i in range(RAW)]
        mraw_in = [sem(f"mraw_in{i}") for i in range(MRAW)]
        x_in = [sem(f"x_in{i}") for i in range(4)]
        x_again = sem("x_again")
        par_in = sem("par_in")
        gain0_in = sem("gain0_in")
        rgw_in = sem("rgw_in")
        hgain_in = sem("hgain_in")
        gains_in = sem("gains_in")
        out_sent = sem("out_sent")
        w_hi, w_lo = sem("w_hi"), sem("w_lo")
        tile_done = sem("tile_done")
        act_free, dve_free = sem("act_free"), sem("dve_free")
        act_step, dve_step, pool_step = sem("act_step"), sem("dve_step"), sem("pool_step")
        const_ready = sem("const_ready")
        par_t = sem("par_t")
        par_ready = sem("par_ready")
        chan_a, chan_d = sem("chan_a"), sem("chan_d")
        rgw_zero = sem("rgw_zero")
        sq_done, rms_done = sem("sq_done"), sem("rms_done")
        mean_ready, half_sum, half_mean = sem("mean_ready"), sem("half_sum"), sem("half_mean")
        gain0_ready = sem("gain0_ready")
        xn_ready, xn_t, h_hi, h_lo = sem("xn_ready"), sem("xn_t"), sem("h_hi"), sem("h_lo")
        rg_conv, rg_gate, rg_raw = sem("rg_conv"), sem("rg_gate"), sem("rg_raw")
        rg_act, rg_dve, ya_hi, ya_lo = sem("rg_act"), sem("rg_dve"), sem("ya_hi"), sem("ya_lo")
        q_ready = sem("q_ready")
        f_act, b_ready = sem("f_act"), sem("b_ready")
        lev_d, lev_e, lev_qe, lev_ke, lev_p, lev_m = (sem(f"lev_{n}") for n in ("d", "e", "qe", "ke", "p", "m"))
        kd_t, kd_ready, kv_done, st_ready, o_done, o_ready = (
            sem(n) for n in ("kd_t", "kd_ready", "kv_done", "st_ready", "o_done", "o_ready"))
        on_a, on_d, g_ready, oc_ready, oc_t, yc_hi, yc_lo = (
            sem(n) for n in ("on_a", "on_d", "g_ready", "oc_ready", "oc_t", "yc_hi", "yc_lo"))
        z_done, sp_ln, sp_ready, sp_masked, suf_done, w_exp, w_ready, av_done, yb_hi, yb_lo = (
            sem(n) for n in ("z_done", "sp_ln", "sp_ready", "sp_masked", "suf_done", "w_exp", "w_ready",
                             "av_done", "yb_hi", "yb_lo"))
        gate_ready, merged_sum, merged_hi, merged_lo = (
            sem(n) for n in ("gate_ready", "merged_sum", "merged_hi", "merged_lo"))
        relu_done, hid_done, hid_hi, hid_lo = (sem(n) for n in ("relu_done", "hid_done", "hid_hi", "hid_lo"))
        y_done = sem("y_done")

        block = ctx.enter_context(nc.Block())

        def free_count(s):
            mine = (s // 4) in BY_ACT
            n = sum(1 for r in range(s + 1) if ((r // 4) in BY_ACT) == mine)
            return (act_free if mine else dve_free), n

        LAST = "last round"

        def rnd(f):
            return NF - 1 if f is LAST else f

        def mlp_tile(f, k):
            if type(f) is int and f == 0 and k in (2, 3):
                return pside[:, 4 + k - 2, :]
            return pmain[:, (NS + k) % 2]

        DVE_FREE0 = sum(1 for r in range(NS) if (r // 4) not in BY_ACT)

        def hi_of(t):
            return t.bitcast(F32)

        @block.sync
        def _(sp):
            def load_unit(U):
                if U >= RAW:
                    sp.wait_ge(w_lo, U - RAW + 1)
                sp.dma_start(raw[:, U % RAW], unit_source(U)).then_inc(raw_in[U % RAW], 16)

            def load_x(t):
                sp.dma_start(xin[:, t], x_v[t]).then_inc(x_in[t], 16)

            load_x(0)
            sp.dma_start(gain0, ln_gains[0, 0:1, :]).then_inc(gain0_in, 16)
            load_unit(0)
            load_x(1)
            load_unit(1)
            load_unit(2)
            load_x(2)
            load_unit(3)
            load_x(3)
            sp.dma_start(par_rows[0:16], conv_w[0].rearrange("k (c p) -> (k c) p", p=P)).then_inc(par_in, 16)
            for i, v in enumerate((conv_b, rg_b_a, rg_b_x, rg_lambda, lb_logits)):
                sp.dma_start(par_rows[16 + 4 * i:20 + 4 * i],
                             v[0].rearrange("(c p) -> c p", p=P)).then_inc(par_in, 16)
            sp.wait_ge(rgw_zero, 1)
            for w, dst in ((rg_w_a, rg_wa), (rg_w_x, rg_wx)):
                for half in range(2):
                    src = w[0].rearrange("(j two) c d -> two c j d", two=2)[half]
                    sp.dma_start(dst[64 * half:64 * half + 64, :, 64 * half:64 * half + 64],
                                 src).then_inc(rgw_in, 16)
            for U in range(RAW, NU):
                if U == FIRST_UNIT[G_GB[1] + 2]:
                    sp.wait_ge(av_done, 8)
                    sp.dma_start(hgain, hgrn_norm[0:1, :].partition_broadcast(P)).then_inc(hgain_in, 16)
                load_unit(U)
            sp.wait_ge(merged_lo, 8)
            for t in range(4):
                sp.dma_start(x1[:, t], x_v[t]).then_inc(x_again, 16)
            for i, g in ((1, gain1), (2, gain2), (3, gain3)):
                sp.dma_start(g, ln_gains[0, i:i + 1, :].partition_broadcast(P)).then_inc(gains_in, 16)

            with sp.Fori(0, NF) as f:
                for g in range(4):
                    for u in range(4):
                        n = 4 * g + u
                        sp.wait_ge(w_lo, 16 * f + (NU + n - MRAW + 1))
                        src = wup_v[f, g, u] if g < 2 else wdn_v[f, g - 2, u]
                        sp.dma_start(mraw[:, n % MRAW], src).then_inc(mraw_in[n % MRAW], 16)
            for t in range(4):
                for half in range(2):
                    c = slice(512 * half, 512 * half + 512)
                    sp.wait_ge(y_done, 2 * t + half + 1)
                    sp.dma_start(out_v[t][:, c], o4[:, t, c]).then_inc(out_sent, 16)
            sp.wait_ge(out_sent, 128)

        @block.gpsimd
        def _(pool):
            count = [0]

            def step(ins):
                count[0] += 1
                ins.then_inc(pool_step, 1)
                pool.wait_ge(pool_step, count[0])

            g = nc.gpsimd
            g.memset(epsb[:], EPS)
            g.memset(ones_row, 1.0)
            step(g.memset(ident[:], 0.0))
            step(g.affine_select(out=ident[:], in_=ident[:], compare_op=ALU.not_equal, fill=1.0, base=0,
                                 pattern=[[-1, P]], channel_multiplier=1))
            g.memset(nones[:], -1.0).then_inc(const_ready, 1)
            step(g.memset(ntri[:], -1.0))
            step(g.affine_select(out=ntri[:], in_=ntri[:], compare_op=ALU.is_ge, fill=0.0, base=0,
                                 pattern=[[-1, P]], channel_multiplier=1))
            step(g.memset(scan_keep[:], 1.0))
            g.memset(scan_keep[:].rearrange("p (c n) -> p c n", n=64)[:, :, 0:1], 0.0).then_inc(const_ready, 1)
            g.memset(rg_wa, 0.0)
            g.memset(rg_wx, 0.0).then_inc(rgw_zero, 1)
            step(g.memset(masks[:], 0))
            for l, m in enumerate(LEVELS):
                second = masks[:, l, :].rearrange("p (b two m) -> p b two m", two=2, m=m)[:, :, 1, :]
                nb = P // (2 * m)
                step(g.memset(second, 1))
                step(g.affine_select(out=second, in_=second, compare_op=ALU.is_ge, fill=0.0, base=0,
                                     pattern=[[-2 * m, nb], [0, m]], channel_multiplier=1))
                last = g.affine_select(out=second, in_=second, compare_op=ALU.is_ge, fill=0.0, base=m - 1,
                                       pattern=[[2 * m, nb], [0, m]], channel_multiplier=-1)
                if l < len(LEVELS) - 1:
                    step(last)
            last.then_inc(const_ready, 1)

            def level_k(h, p):
                if h == 0 and p == 0:
                    pool.wait_ge(f_act, 20)
                for i in range(2):
                    r = 2 * p + i
                    if r == 0:
                        continue
                    pool.wait_ge(lev_e, 7 * h + r)
                    if r >= 3:
                        pool.wait_ge(lev_p, 7 * h + r - 1)
                    elif h:
                        pool.wait_ge(lev_p, 7 * h)
                        pool.wait_ge(kd_t, h)
                    g.tensor_tensor(lev_k[i], hg_k[:, h], lev_q[i], ALU.mult).then_inc(lev_ke, 1)

            def causal(buf, done):
                diag = buf[:, 0:1152].rearrange("p (b n) -> p b n", n=128)[:, 0:9:4, :]
                g.affine_select(out=diag, in_=diag, compare_op=ALU.is_gt, fill=0.0, base=0,
                                pattern=[[0, 3], [1, P]], channel_multiplier=-1)
                g.affine_select(out=buf[:, 896:1024], in_=buf[:, 896:1024], compare_op=ALU.is_gt, fill=0.0,
                                base=0, pattern=[[1, P]], channel_multiplier=-1).then_inc(done, 1)

            for s in range(NS):
                kind, what = GROUPS[s // 4]
                if kind == "br" and what[0]:
                    d = 4 * what[1] + s % 4
                    pool.wait_ge(*free_count(s))
                    g.tensor_tensor(merged[d], merged[d], br_t[d % 2], ALU.add).then_inc(merged_sum, 1)
                for h, b in enumerate(HG_AT):
                    if b <= s < b + 4:
                        level_k(h, s - b)
                for a, b in enumerate(ATT_AT):
                    if s == b:
                        pool.wait_ge(sp_ready, a + 1)
                        causal(stick[a % 2], sp_masked)
                    if s == b + 1:
                        pool.wait_ge(w_exp, a + 1)
                        causal(stick[a % 2], w_ready)

        @block.scalar
        def _(act):
            a_ = nc.scalar
            n = {}

            def mark(ins, s):
                n[s.name] = n.get(s.name, 0) + 1
                ins.then_inc(s, 1)
                n["last"] = (s, n[s.name])

            def after():
                act.wait_ge(*n["last"])

            def step(ins):
                mark(ins, act_step)

            def split_hi(U):
                act.wait_ge(raw_in[U % RAW], 16 * (U // RAW + 1))
                if U >= RING:
                    act.wait_ge(tile_done, 4 * (OWNER[U - RING] + 1))
                mark(a_.activation(whi[:, U % RING], raw[:, U % RAW], ACT.Copy), w_hi)

            def split_hi_mlp(f, u):
                act.wait_ge(mraw_in[u % MRAW], 64 * f + 16 * (u // MRAW + 1))
                act.wait_ge(tile_done, 16 * f + (NS + 4 * (u // 4) - 4))
                a_.activation(whi[:, (NU + u) % RING], mraw[:, u % MRAW], ACT.Copy).then_inc(w_hi, 1)

            loaded = [None]

            def tables(name):
                if loaded[0] != name:
                    a_.preload_act_table_set(name)
                    loaded[0] = name

            def mean_root(t, rest=None):
                mark(a_.activation(ss[:, t:t + 1], ss[:, t:t + 1], ACT.Sqrt, scale=1.0 / D,
                                   bias=epsb[:] if rest is None else rest), rms_done)

            def round_t(dst, t, bank):
                src = pside[:, bank:bank + 2, :].rearrange("p a (b n) -> p (a b) n", n=P)
                mark(a_.activation(dst[:, :, t * P:(t + 1) * P], src, ACT.Copy), h_hi)

            tables(SQRT_SET)
            act.wait_ge(const_ready, 1)
            for t in range(4):
                act.wait_ge(x_in[t], 16)
                step(a_.activation(xsq, xin[:, t], ACT.Square, accum_out=ss[:, t:t + 1]))
                after()
                mean_root(t)
                split_hi(t)
                if t:
                    act.wait_ge(xn_t, t)
                    round_t(hhi, t - 1, 2 * ((t - 1) % 2))
            act.wait_ge(xn_t, 4)
            round_t(hhi, 3, 2)

            def channel_constants():
                act.wait_ge(par_ready, 1)
                tables(EXP_LN_SET)
                step(a_.activation(ca, c_lam, ACT.Abs))
                after()
                step(a_.activation(ca, ca, ACT.Exp, scale=-1.0))
                after()
                mark(a_.activation(ca, ca, ACT.Ln, bias=1.0), chan_a)
                act.wait_ge(chan_d, 2)
                mark(a_.activation(ln1mlb, cb, ACT.Ln, bias=1.0, scale=-1.0), chan_a)
                act.wait_ge(chan_d, 3)
                mark(a_.activation(lnlb, cc, ACT.Ln), chan_a)

            def forget_gate(h):
                ps = pmain[:, (4 * G_F + h) % 2]
                act.wait_ge(chan_d, 5)
                tables(EXP_LN_SET)
                if h:
                    act.wait_ge(b_ready, h)
                else:
                    act.wait_ge(rg_dve, 8)
                step(a_.activation(f0, ps, ACT.Abs))
                after()
                step(a_.activation(f0, f0, ACT.Exp, scale=-1.0))
                after()
                mark(a_.activation(f0, f0, ACT.Ln, bias=1.0), f_act)
                act.wait_ge(*free_count(4 * G_F + h))
                mark(a_.activation(f0, f1, ACT.Abs, bias=ln_diff[:, h:h + 1]), f_act)
                after()
                mark(a_.activation(f0, f0, ACT.Exp, scale=-1.0), f_act)
                mark(a_.activation(hg_k[:, h], f2, ACT.Exp, scale=-1.0, bias=ln1mlb[:, h:h + 1]), f_act)
                after()
                mark(a_.activation(f0, f0, ACT.Ln, bias=1.0), f_act)

            def halves(buf, m):
                v = buf.rearrange("p (b two m) -> p b two m", two=2, m=m)
                return v[:, :, 0, :], v[:, :, 1, :]

            def level_exp(h, p):
                for i in range(2):
                    r = 2 * p + i
                    if r == 0:
                        continue
                    act.wait_ge(lev_d, 7 * h + r)
                    if r == 7:
                        mark(a_.activation(lev_q[i], lev_q[i], ACT.Exp, scale=-1.0), lev_e)
                    else:
                        first, second = halves(lev_q[i], LEVELS[r - 1])
                        a_.activation(first, first, ACT.Exp, scale=-1.0)
                        mark(a_.activation(second, second, ACT.Exp), lev_e)
                if p == 3:
                    if h:
                        act.wait_ge(o_done, h)
                        act.wait_ge(st_ready, 7 * h)
                    step(a_.activation(dec[:], hg_b[:, h].rearrange("p (c n) -> p c n", n=64)[:, :, 63], ACT.Exp))
                    mark(a_.activation(qb, hg_b[:, h], ACT.Exp), kd_ready)

            for s in range(NS):
                g, j = divmod(s, 4)
                for U in SPLIT_AT[s]:
                    if U < NU:
                        split_hi(U)
                    else:
                        split_hi_mlp(0, U - NU)
                for h, b in enumerate(HG_AT):
                    if b <= s < b + 4:
                        level_exp(h, s - b)
                ps = pmain[:, s % 2]
                if g in BY_ACT or g == G_F:
                    act.wait_ge(tile_done, s + 1)
                if g == G_Q:
                    mark(a_.activation(hg_q[:, j], ps, ACT.Copy), act_free)
                    if j == 3:
                        after()
                        tables(SILU_SET)
                        mark(a_.activation(hg_q, hg_q, ACT.Silu), q_ready)
                if g == G_F:
                    forget_gate(j)
                if g == G_I:
                    mark(a_.activation(hg_v[:, j], ps, ACT.Copy), act_free)
                    if j == 3:
                        channel_constants()
                if g == G_SQ:
                    act.wait_ge(ya_lo, 1)
                    mark(a_.activation(sb_q[:, j], ps, ACT.Copy, scale=0.125), act_free)
                if g == G_SK:
                    mark(a_.activation(sb_k[:, j], ps, ACT.Copy), act_free)
                if g == G_SV:
                    mark(a_.activation(sb_v[:, j], ps, ACT.Copy), act_free)

                if s == RG_AT + 6:
                    act.wait_ge(rg_raw, 8)
                    tables(SIGMOID_SET)
                    step(a_.activation(rg_ri, rg_ri, ACT.Sigmoid))
                    after()
                    tables(EXP_SET)
                    for j4 in range(4):
                        mark(a_.activation(rg_a[:, j4], rg_ri[:, j4], ACT.Exp, scale=c8[:, j4:j4 + 1]), rg_act)
                    after()
                    for j4 in range(4):
                        mark(a_.activation(rg_ri[:, j4], rg_ri[:, j4], ACT.Tanh, scale=c8n[:, j4:j4 + 1]), rg_act)
                if s == RG_AT + 7:
                    act.wait_ge(rg_dve, 2)
                    tables(SQRT_SET)
                    mark(a_.activation(rg_ri[:, 0:4], rg_ri[:, 0:4], ACT.Sqrt), rg_act)
                    act.wait_ge(rg_dve, 8)
                    mark(a_.activation(yhi[:, 0:4], rg_ri[:, 0:4], ACT.Copy), ya_hi)

                for h, b in enumerate(HG_AT):
                    if s == b + 3:
                        act.wait_ge(kd_t, h + 1)
                        if h:
                            act.wait_ge(kv_done, h)
                        mark(a_.activation(kdt, pside[:, 0, :].rearrange("p (a b) -> p a b", b=P), ACT.Copy), kd_ready)

                for a, b in enumerate(ATT_AT):
                    if s == b:
                        buf = stick[a % 2]
                        act.wait_ge(z_done, a + 1)
                        tables(EXP_LN_SET)
                        if a >= 2:
                            act.wait_ge(av_done, a - 1)
                        elif a == 0:
                            act.wait_ge(lev_p, 28)
                            act.wait_ge(kd_t, 4)
                        else:
                            act.wait_ge(o_done, 4)
                        step(a_.activation(buf, pz[:, 0:1280], ACT.Abs))
                        after()
                        step(a_.activation(buf, buf, ACT.Exp, scale=-1.0))
                        after()
                        mark(a_.activation(buf, buf, ACT.Ln, bias=1.0), sp_ln)
                    if s == b + 1:
                        act.wait_ge(suf_done, a + 1)
                        tables(EXP_LN_SET)
                        mark(a_.activation(stick[a % 2], pz[:, 0:1280], ACT.Exp), w_exp)
                    if s == b + 2 and a % 2:
                        act.wait_ge(av_done, a + 1)
                        mark(a_.activation(yhi[:, 4 + a // 2], pyb, ACT.Copy), yb_hi)

                for k, gg in enumerate((*G_GA, *G_GB, *G_GC)):
                    if s == 4 * gg + 3:
                        act.wait_ge(dve_free, free_count(s)[1])
                        buf = gates[k]
                        tables(SIGMOID_SET)
                        mark(a_.activation(buf, buf, ACT.Sigmoid), gate_ready)
                if s == 4 * G_G + 3:
                    act.wait_ge(dve_free, free_count(s)[1])
                    tables(SILU_SET)
                    mark(a_.activation(hg_g, hg_g, ACT.Silu), g_ready)

                if s == ON_AT:
                    act.wait_ge(o_ready, 4)
                    act.wait_ge(av_done, 8)
                    for i in range(16):
                        t, h = divmod(i, 4)
                        step(a_.activation(hg_sq, hg_v[:, t, h * P:(h + 1) * P], ACT.Square,
                                           accum_out=hg_ss[:, i:i + 1]))
                        after()
                    tables(SQRT_SET)
                    mark(a_.activation(hg_ss[:], hg_ss[:], ACT.Sqrt, bias=epsb[:], scale=1.0 / P), on_a)
                for t in range(4):
                    if s == YC_AT + t:
                        act.wait_ge(oc_t, t + 1)
                        mark(a_.activation(yhi[:, 0:4, t * P:(t + 1) * P],
                                           pside[:, t % 2].rearrange("p (a b) -> p a b", b=P), ACT.Copy), yc_hi)

                if GROUPS[g][0] == "br" and GROUPS[g][1][0] == 2:
                    d = 4 * GROUPS[g][1][1] + j
                    act.wait_ge(merged_sum, 8 + d + 1)
                    mark(a_.activation(hhi[:, d], merged[d], ACT.Copy), merged_hi)

                if g in G_OUT:
                    half = g - G_OUT[0]
                    if half == 0 and j == 0:
                        act.wait_ge(merged_lo, 8)
                        tables(SQRT_SET)
                    part = o4[:, j, 512 * half:512 * half + 512]
                    mark(a_.activation(part, ps, ACT.Copy), act_free)
                    after()
                    if half == 0:
                        mark(a_.activation(sq[:, 0:512], part, ACT.Square, accum_out=ss_half[:, j:j + 1]), half_sum)
                        after()
                    else:
                        step(a_.activation(sq[:, 0:512], part, ACT.Square, accum_out=ss[:, j:j + 1]))
                        after()
                        act.wait_ge(half_mean, j + 1)
                        mean_root(j, ms_half[:, j:j + 1])
                        act.wait_ge(mean_ready, 2 * j + 2)
                        step(a_.activation(sq, x1[:, j], ACT.Square, accum_out=ss[:, j:j + 1]))
                        after()
                        mean_root(j)
                        if j >= 2:
                            act.wait_ge(xn_t, 4 + j - 1)
                            round_t(yhi, j - 2, 2 * (j % 2))

            for t in (2, 3):
                act.wait_ge(xn_t, 4 + t + 1)
                round_t(yhi, t, 2 * (t % 2))

            def mlp(f, g):
                for j in range(4):
                    k = 4 * g + j
                    if f is not LAST or g < 3:
                        split_hi_mlp(rnd(f), k + 4)
                    act.wait_ge(tile_done, 16 * rnd(f) + (NS + k + 1))
                    if g < 2:
                        if k >= 2:
                            act.wait_ge(hid_done, 8 * rnd(f) + (k - 1))
                        a_.activation(relu[k % 2], mlp_tile(f, k), ACT.Relu).then_inc(relu_done, 1)
                        act.wait_ge(hid_done, 8 * rnd(f) + (k + 1))
                        a_.activation(hhi[:, k], hid[k % 2], ACT.Copy).then_inc(hid_hi, 1)
                    elif f is LAST:
                        half = g - 2
                        act.wait_ge(dve_free, DVE_FREE0 + 8 * (NF - 1) + 4 * half + j + 1)
                        part = o4[:, j, 512 * half:512 * half + 512]
                        if half == 0:
                            mark(a_.activation(sq[:, 0:512], part, ACT.Square, accum_out=ss_half[:, j:j + 1]), half_sum)
                            after()
                        else:
                            step(a_.activation(sq[:, 0:512], part, ACT.Square, accum_out=ss[:, j:j + 1]))
                            after()
                            act.wait_ge(half_mean, 4 + j + 1)
                            mean_root(j, ms_half[:, j:j + 1])

            mlp(0, 0)
            with act.Fori(0, NF - 1) as f:
                for g in (1, 2, 3):
                    mlp(f, g)
                mlp(f + 1, 0)
            for g in (1, 2, 3):
                mlp(LAST, g)

        @block.vector
        def _(dve):
            v = nc.vector
            n = {}

            def mark(ins, s):
                n[s.name] = n.get(s.name, 0) + 1
                ins.then_inc(s, 1)
                n["last"] = (s, n[s.name])

            def after():
                dve.wait_ge(*n["last"])

            def step(ins):
                mark(ins, dve_step)

            def split_lo(U):
                dve.wait_ge(w_hi, U + 1)
                mark(v.tensor_tensor(wlo[:, U % RING], raw[:, U % RAW], whi[:, U % RING].bitcast(F32), ALU.subtract), w_lo)

            def split_lo_mlp(f, u):
                dve.wait_ge(w_hi, 16 * f + (NU + u + 1))
                v.tensor_tensor(wlo[:, (NU + u) % RING], mraw[:, u % MRAW],
                                whi[:, (NU + u) % RING].bitcast(F32), ALU.subtract).then_inc(w_lo, 1)

            def take(dst, s):
                dve.wait_ge(tile_done, s + 1)
                mark(v.tensor_copy(dst, pmain[:, s % 2]), dve_free)

            def half_to_mean(t, n_sums):
                dve.wait_ge(half_sum, n_sums)
                mark(v.tensor_scalar(ms_half[:, t:t + 1], ss_half[:, t:t + 1], 1.0 / D, EPS, ALU.mult, ALU.add), half_mean)

            def norm_scale(dst, src, t, gain, done):
                step(v.reciprocal(rstd[:, t:t + 1], ss[:, t:t + 1]))
                after()
                mark(v.scalar_tensor_tensor(dst, src, rstd[:, t:t + 1], gain, ALU.mult, ALU.mult), done)

            def rest_t(hi, lo, t, bank):
                src = pside[:, bank:bank + 2, :].rearrange("p a (b n) -> p (a b) n", n=P)
                mark(v.tensor_tensor(lo[:, :, t * P:(t + 1) * P], src, hi[:, :, t * P:(t + 1) * P].bitcast(F32),
                                     ALU.subtract), h_lo)

            g0 = pside[:, 4:6, :].rearrange("p a n -> p (a n)")
            dve.wait_ge(gain0_ready, 1)
            for t in range(4):
                dve.wait_ge(rms_done, t + 1)
                if t >= 2:
                    dve.wait_ge(xn_t, t - 1)
                norm_scale(xn[t % 2], xin[:, t], t, g0, xn_ready)
                split_lo(t)
                if t:
                    dve.wait_ge(h_hi, t)
                    rest_t(hhi, hlo, t - 1, 2 * ((t - 1) % 2))
            dve.wait_ge(h_hi, 4)
            rest_t(hhi, hlo, 3, 2)

            def channel_constants():
                dve.wait_ge(par_t, 1)
                mark(v.tensor_copy(par[:], ph[0][:, 0:NPAR]), par_ready)
                after()
                dve.wait_ge(chan_a, 1)
                step(v.tensor_scalar(cb, c_lam, 0.0, None, ALU.min))
                after()
                step(v.tensor_tensor(ca, ca, cb, ALU.subtract))
                after()
                step(v.tensor_scalar(c8n, ca, RG_C, None, ALU.mult))
                mark(v.tensor_scalar(c8, ca, -RG_C, None, ALU.mult), chan_d)
                after()
                step(v.tensor_tensor(cb, c_lb, c_lb, ALU.subtract))
                after()
                step(v.tensor_scalar(cc, cb, 1.0, None, ALU.add))
                after()
                mark(v.tensor_tensor(cb, cc, cc, ALU.subtract), chan_d)
                after()
                mark(v.tensor_scalar(cc, cb, LB_FLOOR, 2.0 ** 50, ALU.max, ALU.mult), chan_d)
                dve.wait_ge(chan_a, 3)
                mark(v.tensor_scalar(lnlb, lnlb, -50.0 * 0.6931471805599453, None, ALU.add), chan_d)
                after()
                mark(v.tensor_tensor(ln_diff, ln1mlb, lnlb, ALU.subtract), chan_d)
                step(v.memset(rg_xp[:, :, 0:3], 0.0))
                after()

            def rg_bias(j):
                dve.wait_ge(rg_gate, j + 1)
                mark(v.tensor_scalar(rg_ri[:, j], ph[0], c_ba[:, j:j + 1], None, ALU.add), rg_raw)
                mark(v.tensor_scalar(rg_ri[:, 4 + j], ph[1], c_bx[:, j:j + 1], None, ALU.add), rg_raw)

            def forget_gate(h):
                ps = pmain[:, (4 * G_F + h) % 2]
                dve.wait_ge(f_act, 5 * h + 1)
                mark(v.scalar_tensor_tensor(f1, ps, 0.0, f0, ALU.min, ALU.subtract), dve_step)
                mark(v.scalar_tensor_tensor(f2, ps, 0.0, f0, ALU.max, ALU.add), dve_free)
                after()
                dve.wait_ge(f_act, 5 * h + 2)
                step(v.tensor_scalar(f1, f1, ln1mlb[:, h:h + 1], lnlb[:, h:h + 1], ALU.add, ALU.max))
                after()
                dve.wait_ge(f_act, 5 * h + 5)
                step(v.tensor_tensor(f1, f1, f0, ALU.add))
                after()
                mark(v.tensor_tensor_scan(hg_b[:, h], scan_keep[:], f1, 0.0, ALU.mult, ALU.add), b_ready)

            def level_prep(h, p):
                for i in range(2):
                    r = 2 * p + i
                    if r == 0:
                        continue
                    if 8 * h + r >= 2:
                        prev = 8 * h + r - 2
                        if prev % 8 == 7:
                            dve.wait_ge(lev_ke, 7 * (prev // 8 + 1))
                        elif prev % 8:
                            dve.wait_ge(lev_p, 7 * (prev // 8) + prev % 8 + 1)
                    if r == 7:
                        b64 = hg_b[:, h].rearrange("p (c n) -> p c n", n=64)
                        mark(v.tensor_tensor(lev_q[i].rearrange("p (c n) -> p c n", n=64), b64,
                                             b64[:, :, 63:64].to_broadcast((P, 8, 64)), ALU.subtract), lev_d)
                    else:
                        m = LEVELS[r - 1]
                        bb = hg_b[:, h].rearrange("p (c n) -> p c n", n=2 * m)
                        mark(v.tensor_tensor(lev_q[i].rearrange("p (c n) -> p c n", n=2 * m), bb,
                                             bb[:, :, m - 1:m].to_broadcast((P, S // (2 * m), 2 * m)),
                                             ALU.subtract), lev_d)
                for i in range(2):
                    r = 2 * p + i
                    if r in (0, 7):
                        continue
                    dve.wait_ge(lev_ke, 7 * h + r)
                    mark(v.tensor_tensor(lev_q[i], hg_q[:, h], lev_q[i], ALU.mult), lev_qe)
                if p == 3:
                    dve.wait_ge(kd_ready, 2 * h + 1)
                    mark(v.tensor_tensor(qb, hg_q[:, h], qb, ALU.mult), lev_qe)

            def merged_rest(d):
                dve.wait_ge(merged_hi, d + 1)
                mark(v.tensor_tensor(hlo[:, d], merged[d], hhi[:, d].bitcast(F32), ALU.subtract), merged_lo)

            def level_merge(h, p):
                for i in range(2):
                    r = 2 * p + i
                    if r == 7:
                        continue
                    dve.wait_ge(lev_p, 7 * h + r + 1)
                    ps = ph[i].rearrange("p (a b) -> p a b", b=P)
                    if r == 0:
                        if h:
                            dve.wait_ge(kv_done, h)
                        mark(v.tensor_tensor(attn_t, ps, ident[:].unsqueeze(1).to_broadcast((P, 4, P)), ALU.mult), lev_m)
                    else:
                        after()
                        mark(v.copy_predicated(attn_t, masks[:, r - 1:r, :].to_broadcast((P, 4, P)), ps), lev_m)

            for s in range(NS):
                g, j = divmod(s, 4)
                for U in SPLIT_AT[s]:
                    split_lo(U) if U < NU else split_lo_mlp(0, U - NU)
                for h, b in enumerate(HG_AT):
                    if b <= s < b + 4:
                        if s == HG_AT[0]:
                            dve.wait_ge(q_ready, 1)
                            dve.wait_ge(b_ready, 4)
                        level_prep(h, s - b)

                ps = pmain[:, s % 2]
                if s == 3:
                    channel_constants()
                if g == G_RG:
                    take(rg_xp[:, j, 3:XPW], s)
                    after()
                    step(v.tensor_scalar(rg_xc[:, j], rg_xp[:, j, 0:512], c_conv(0, j), c_convb[:, j:j + 1],
                                         ALU.mult, ALU.add))
                    for k in range(1, 4):
                        after()
                        ins = v.scalar_tensor_tensor(rg_xc[:, j], rg_xp[:, j, k:k + 512], c_conv(k, j), rg_xc[:, j],
                                                     ALU.mult, ALU.add)
                        mark(ins, rg_conv) if k == 3 else step(ins)
                if RG_AT + 2 <= s < RG_AT + 6:
                    rg_bias(s - RG_AT - 2)
                if s == RG_AT + 6:
                    dve.wait_ge(rg_act, 4)
                    mark(v.tensor_tensor(rg_t, rg_a, rg_a, ALU.mult), rg_dve)
                    after()
                    dve.wait_ge(rg_act, 8)
                    step(v.scalar_tensor_tensor(rg_ri[:, 0:4], rg_t, 1.0, rg_ri[:, 0:4], ALU.add, ALU.mult))
                    after()
                    mark(v.tensor_scalar(rg_ri[:, 0:4], rg_ri[:, 0:4], 0.0, None, ALU.max), rg_dve)
                    step(v.tensor_tensor(rg_t, rg_ri[:, 4:8], rg_xc, ALU.mult))
                    after()
                if s == RG_AT + 7:
                    dve.wait_ge(rg_act, 9)
                    mark(v.memset(rg_ri[:, 0:4, 0:1], 1.0), rg_dve)
                    after()
                    mark(v.tensor_tensor(rg_t, rg_t, rg_ri[:, 0:4], ALU.mult), rg_dve)
                    after()
                    for j4 in range(4):
                        mark(v.tensor_tensor_scan(rg_ri[:, j4], rg_a[:, j4], rg_t[:, j4], 0.0,
                                                  ALU.mult, ALU.add), rg_dve)
                    dve.wait_ge(ya_hi, 1)
                    mark(v.tensor_tensor(ylo[:, 0:4], rg_ri[:, 0:4], yhi[:, 0:4].bitcast(F32), ALU.subtract), ya_lo)
                if g == G_F:
                    dve.wait_ge(tile_done, s + 1)
                    forget_gate(j)

                for h, b in enumerate(HG_AT):
                    if b <= s < b + 4:
                        level_merge(h, s - b)
                    if s == b + 4:
                        dve.wait_ge(kv_done, h + 1)
                        if h:
                            dve.wait_ge(o_done, h)
                        for c in range(7):
                            kv = pside[:, 1 + c % 2, (c // 2) * P:(c // 2 + 1) * P]
                            if c == 0:
                                mark(v.tensor_copy(states[:, 0], kv), st_ready)
                            else:
                                after()
                                mark(v.scalar_tensor_tensor(states[:, c], states[:, c - 1], dec[:, c:c + 1], kv,
                                                            ALU.mult, ALU.add), st_ready)
                    if s == b + 5:
                        dve.wait_ge(o_done, h + 1)
                        mark(v.tensor_copy(hg_v[:, :, h * P:(h + 1) * P], pyb.rearrange("p (a b) -> p a b", b=P)), o_ready)

                for k, gg in enumerate((*G_GA, *G_GB, *G_GC)):
                    if g == gg:
                        if gg == G_GB[1] and j == 0:
                            dve.wait_ge(z_done, 8)
                        if gg == G_GA[0] and j in (0, 3):
                            dve.wait_ge(lev_ke, 21 if j == 0 else 28)
                        if gg == G_GA[1] and j == 0:
                            dve.wait_ge(lev_qe, 28)
                        take(gates[k][:, j], s)
                if g == G_G:
                    if j == 0:
                        dve.wait_ge(z_done, 8)
                    take(hg_g[:, j], s)

                for a, b in enumerate(ATT_AT):
                    if s == b:
                        dve.wait_ge(sp_ln, a + 1)
                        mark(v.scalar_tensor_tensor(stick[a % 2], pz[:, 0:1280], 0.0, stick[a % 2],
                                                    ALU.max, ALU.add), sp_ready)
                    if s == b + 2 and a % 2:
                        dve.wait_ge(yb_hi, a // 2 + 1)
                        mark(v.tensor_tensor(ylo[:, 4 + a // 2], pyb, yhi[:, 4 + a // 2].bitcast(F32), ALU.subtract), yb_lo)

                if GROUPS[g][0] == "br":
                    branch, half = GROUPS[g][1]
                    d = 4 * half + j
                    dve.wait_ge(gate_ready, 2 * branch + half + 1)
                    gate = gates[2 * branch + half][:, j]
                    dve.wait_ge(tile_done, s + 1)
                    if branch == 0:
                        mark(v.tensor_tensor(merged[d], ps, gate, ALU.mult), dve_free)
                    else:
                        if d >= 2 or branch == 2:
                            dve.wait_ge(merged_sum, 8 * (branch - 1) + d - 1)
                        mark(v.tensor_tensor(br_t[d % 2], ps, gate, ALU.mult), dve_free)
                    if branch == 2 and d:
                        merged_rest(d - 1)

                if s == ON_AT + 1:
                    dve.wait_ge(on_a, 1)
                    dve.wait_ge(hgain_in, 16)
                    step(v.reciprocal(hg_rstd[:], hg_ss[:]))
                    after()
                    for i in range(16):
                        t, h = divmod(i, 4)
                        o = hg_v[:, t, h * P:(h + 1) * P]
                        mark(v.scalar_tensor_tensor(o, o, hg_rstd[:, i:i + 1], hgain, ALU.mult, ALU.mult), on_d)
                if s == 4 * G_G + 3:
                    dve.wait_ge(g_ready, 1)
                    for t in range(4):
                        mark(v.tensor_tensor(hg_v[:, t], hg_v[:, t], hg_g[:, t], ALU.mult), oc_ready)
                if s == 4 * G_OUT[0]:
                    merged_rest(7)
                for t in range(4):
                    if s == YC_AT + t:
                        dve.wait_ge(yc_hi, t + 1)
                        mark(v.tensor_tensor(ylo[:, 0:4, t * P:(t + 1) * P],
                                             pside[:, t % 2].rearrange("p (a b) -> p a b", b=P),
                                             yhi[:, 0:4, t * P:(t + 1) * P].bitcast(F32), ALU.subtract), yc_lo)

                if g == G_OUT[0]:
                    half_to_mean(j, j + 1)
                if g == G_OUT[1]:
                    if j == 0:
                        dve.wait_ge(gains_in, 48)
                        dve.wait_ge(x_again, 64)
                    dve.wait_ge(rms_done, 4 + 2 * j + 1)
                    norm_scale(o4[:, j], o4[:, j], j, gain1, mean_ready)
                    after()
                    mark(v.tensor_tensor(x1[:, j], x1[:, j], o4[:, j], ALU.add), mean_ready)
                    dve.wait_ge(rms_done, 4 + 2 * j + 2)
                    norm_scale(o4[:, j], x1[:, j], j, gain2, xn_ready)
                    if j >= 2:
                        dve.wait_ge(h_hi, 4 + j - 1)
                        rest_t(yhi, ylo, j - 2, 2 * (j % 2))

            for t in (2, 3):
                dve.wait_ge(h_hi, 4 + t + 1)
                rest_t(yhi, ylo, t, 2 * (t % 2))
            after()
            step(v.memset(o4, 0.0))
            after()

            def mlp(f, g):
                for j in range(4):
                    k = 4 * g + j
                    if f is not LAST or g < 3:
                        split_lo_mlp(rnd(f), k + 4)
                    if g < 2:
                        dve.wait_ge(relu_done, 8 * rnd(f) + (k + 1))
                        if k >= 2:
                            dve.wait_ge(hid_lo, 8 * rnd(f) + (k - 1))
                        v.scalar_tensor_tensor(hid[k % 2], mlp_tile(f, k), 0.0, relu[k % 2],
                                               ALU.max, ALU.mult).then_inc(hid_done, 1)
                        dve.wait_ge(hid_hi, 8 * rnd(f) + (k + 1))
                        v.tensor_tensor(hlo[:, k], hid[k % 2], hhi[:, k].bitcast(F32), ALU.subtract).then_inc(hid_lo, 1)
                    else:
                        half = g - 2
                        part = o4[:, j, 512 * half:512 * half + 512]
                        dve.wait_ge(tile_done, 16 * rnd(f) + (NS + k + 1))
                        v.tensor_tensor(part, part, mlp_tile(f, k), ALU.add).then_inc(dve_free, 1)
                        if f is LAST and half == 0:
                            half_to_mean(j, 4 + j + 1)
                        if f is LAST and half == 1:
                            dve.wait_ge(rms_done, 12 + j + 1)
                            step(v.reciprocal(rstd[:, j:j + 1], ss[:, j:j + 1]))
                            after()
                            for c in (slice(0, 512), slice(512, 1024)):
                                step(v.scalar_tensor_tensor(o4[:, j, c], o4[:, j, c], rstd[:, j:j + 1], gain3[:, c],
                                                            ALU.mult, ALU.mult))
                                after()
                                mark(v.tensor_tensor(o4[:, j, c], o4[:, j, c], x1[:, j, c], ALU.add), y_done)

            mlp(0, 0)
            with dve.Fori(0, NF - 1) as f:
                for g in (1, 2, 3):
                    mlp(f, g)
                mlp(f + 1, 0)
            for g in (1, 2, 3):
                mlp(LAST, g)

        @block.tensor
        def _(pe):
            mm = nc.tensor.matmul

            def product(dst, left, right, k, last_k):
                mm(dst, left[0], right[0], start=(k == 0), stop=False)
                mm(dst, left[0], right[1], start=False, stop=False)
                return mm(dst, left[1], right[0], start=False, stop=(k == last_k))

            def ring(U0, k):
                U = (U0 + k // 2) % RING
                return whi[:, U, k % 2], wlo[:, U, k % 2]

            def transposes(src, dst_bank, nk):
                for k in range(nk):
                    last = nc.tensor.transpose(pside[:, dst_bank + k // 4, (k % 4) * P:(k % 4 + 1) * P],
                                               src[:, k * P:(k + 1) * P], ident[:])
                return last

            pe.wait_ge(const_ready, 1)
            pe.wait_ge(gain0_in, 16)
            for c in range(2):
                last = mm(pside[:, 4 + c, :], ones_row, gain0[:, 512 * c:512 * c + 512], start=True, stop=True)
            last.then_inc(gain0_ready, 1)

            def h_tile(t):
                pe.wait_ge(xn_ready, t + 1)
                if t >= 2:
                    pe.wait_ge(h_lo, t - 1)
                transposes(xn[t % 2], 2 * (t % 2), 8).then_inc(xn_t, 1)

            def main(s):
                g, j = divmod(s, 4)
                kind = GROUPS[g][0]
                if s >= 2:
                    pe.wait_ge(*free_count(s - 2))
                dst = pmain[:, s % 2]
                nk = 4 if kind == "br" else 8
                y0 = 0 if kind != "br" else (0, 4, 0)[GROUPS[g][1][0]]
                for k in range(nk):
                    if j == 0 and k % 2 == 0:
                        pe.wait_ge(w_lo, FIRST_UNIT[g] + k // 2 + 1)
                    if kind == "out" and s == 4 * G_OUT[0]:
                        pe.wait_ge(merged_lo, k + 1)
                    w = ring(FIRST_UNIT[g], k)
                    if kind in ("feat", "br"):
                        left = tuple(x[:, j * P:(j + 1) * P] for x in w)
                        right = (hhi[:, k], hlo[:, k]) if kind == "feat" else (yhi[:, y0 + k], ylo[:, y0 + k])
                    else:
                        left = (hhi[:, k, j * P:(j + 1) * P], hlo[:, k, j * P:(j + 1) * P])
                        right = w
                    last = product(dst, left, right, k, nk - 1)
                last.then_inc(tile_done, 1)

            def rg_gates(j):
                pe.wait_ge(rg_conv, j + 1)
                if j == 0:
                    pe.wait_ge(rgw_in, 64)
                    pe.wait_ge(par_ready, 1)
                else:
                    pe.wait_ge(rg_raw, 2 * j)
                mm(ph[0], rg_wa[:, j], rg_xc[:, j], start=True, stop=True)
                mm(ph[1], rg_wx[:, j], rg_xc[:, j], start=True, stop=True).then_inc(rg_gate, 1)

            def levels(h, p):
                for i in range(2):
                    r = 2 * p + i
                    if r == 7:
                        pe.wait_ge(lev_ke, 7 * h + 7)
                        if h:
                            pe.wait_ge(kd_ready, 2 * h)
                        transposes(lev_k[1], 0, 4).then_inc(kd_t, 1)
                        continue
                    if r == 0:
                        pe.wait_ge(b_ready, h + 1)
                        pe.wait_ge(q_ready, 1)
                        kk, qq = hg_k[:, h], hg_q[:, h]
                    else:
                        pe.wait_ge(lev_ke, 7 * h + r)
                        pe.wait_ge(lev_qe, 7 * h + r)
                        kk, qq = lev_k[i], lev_q[i]
                    if h == 0 and r < 2:
                        pe.wait_ge(rg_raw, 8)
                    else:
                        pe.wait_ge(lev_m, 7 * h + max(r - 1, 0))
                    for t in range(4):
                        c = slice(t * P, (t + 1) * P)
                        last = mm(ph[i][:, c], kk[:, c], qq[:, c], start=True, stop=True)
                    last.then_inc(lev_p, 1)

            def chunk_products(h):
                pe.wait_ge(lev_m, 7 * (h + 1))
                pe.wait_ge(kd_ready, 2 * h + 2)
                if h:
                    pe.wait_ge(o_ready, h)
                    pe.wait_ge(st_ready, 7 * h)
                else:
                    pe.wait_ge(act_free, free_count(4 * G_I + 3)[1])
                for t in range(4):
                    mm(pyb[:, t * P:(t + 1) * P], attn_t[:, t], hg_v[:, t, h * P:(h + 1) * P],
                       start=(t == 0), stop=False, skip_group_check=True)
                for c in range(7):
                    rows = slice(64 * (c % 2), 64 * (c % 2) + 64)
                    last = mm(pside[:, 1 + c % 2, (c // 2) * P:(c // 2 + 1) * P], kdt[rows, c // 2],
                              hg_v[rows, c // 2, h * P:(h + 1) * P], start=True, stop=True)
                last.then_inc(kv_done, 1)

            def state_products(h):
                pe.wait_ge(st_ready, 7 * (h + 1))
                pe.wait_ge(lev_qe, 7 * (h + 1))
                for c in range(1, 8):
                    rows = slice(64 * (c % 2), 64 * (c % 2) + 64)
                    last = mm(pyb[rows, (c // 2) * P:(c // 2 + 1) * P], qb[:, 64 * c:64 * c + 64],
                              states[:, c - 1], start=False, stop=(c == 7), skip_group_check=True)
                last.then_inc(o_done, 1)

            Z_AT = (0, 512, 1024, 896)

            def att_z(a):
                rows = slice(64 * (a % 2), 64 * (a % 2) + 64)
                if a == 0:
                    pe.wait_ge(act_free, free_count(4 * G_SV + 3)[1])
                    pe.wait_ge(st_ready, 28)
                    pe.wait_ge(kd_ready, 8)
                else:
                    pe.wait_ge(w_exp, a)
                for b in (0, 1, 3, 2):
                    last = mm(pz[:, Z_AT[b]:Z_AT[b] + S - P * b], sb_k[rows, a // 2, b * P:(b + 1) * P],
                              sb_q[rows, a // 2, b * P:S], start=(b != 3), stop=False, skip_group_check=True)
                last.then_inc(z_done, 1)

            def att_suffix(a):
                pe.wait_ge(sp_masked, a + 1)
                sp_ = stick[a % 2]
                for b in range(4):
                    for c in range(b, 4):
                        last = mm(pz[:, Z_AT[b] + P * (c - b):Z_AT[b] + S - P * b],
                                  ntri[:] if c == b else nones[:], sp_[:, Z_AT[c]:Z_AT[c] + S - P * c],
                                  start=False, stop=(c == 3), skip_group_check=True)
                last.then_inc(suf_done, 1)

            def att_out(a):
                pe.wait_ge(w_ready, a + 1)
                if a == 0:
                    pe.wait_ge(o_ready, 4)
                elif a % 2 == 0:
                    pe.wait_ge(yb_lo, a // 2)
                rows = slice(64 * (a % 2), 64 * (a % 2) + 64)
                for b in range(4):
                    last = mm(pyb[rows, b * P:S], sb_v[:, b, 64 * a:64 * a + 64],
                              stick[a % 2][:, Z_AT[b]:Z_AT[b] + S - P * b],
                              start=(b == 0), stop=(b == 3), skip_group_check=True)
                last.then_inc(av_done, 1)

            def h2_tile(t):
                pe.wait_ge(xn_ready, 4 + t + 1)
                if t >= 2:
                    pe.wait_ge(h_lo, 4 + t - 1)
                transposes(o4[:, t], 2 * (t % 2), 8).then_inc(xn_t, 1)

            for s in range(NS):
                if s == 4 * 8:
                    pe.wait_ge(ya_lo, 1)
                if s == 4 * 13:
                    pe.wait_ge(yb_lo, 4)
                if s == 4 * 18:
                    pe.wait_ge(yc_lo, 4)
                if s == 0:
                    h_tile(0)
                if s < 4:
                    if s < 3:
                        h_tile(s + 1)
                    else:
                        pe.wait_ge(par_in, 96)
                        pe.wait_ge(xn_ready, 4)
                        nc.tensor.transpose(ph[0][:, 0:NPAR], par_rows[0:NPAR, :],
                                            ident[0:NPAR, 0:NPAR]).then_inc(par_t, 1)
                    pe.wait_ge(h_lo, s + 1)
                main(s)
                if RG_AT + 2 <= s < RG_AT + 6:
                    rg_gates(s - RG_AT - 2)
                for h, b in enumerate(HG_AT):
                    if s == b + 4:
                        chunk_products(h)
                for h, b in enumerate(HG_AT):
                    if b <= s < b + 4:
                        levels(h, s - b)
                    if s == b + 5:
                        state_products(h)
                for a, b in enumerate(ATT_AT):
                    if s == b + 2:
                        att_out(a)
                for a, b in enumerate(ATT_AT):
                    if s == b:
                        att_z(a)
                    if s == b + 1:
                        att_suffix(a)
                for t in range(4):
                    if s == YC_AT + t:
                        pe.wait_ge(oc_ready, t + 1)
                        if t >= 2:
                            pe.wait_ge(yc_lo, t - 1)
                        transposes(hg_v[:, t], t % 2, 4).then_inc(oc_t, 1)
                if s >= NS - 2:
                    h2_tile(s - (NS - 2))

            def mlp(f, g):
                for j in range(4):
                    k = 4 * g + j
                    if k in (0, 1):
                        pe.wait_ge(dve_free, 8 * rnd(f) + (DVE_FREE0 - 1 + k))
                    elif k < 10:
                        pe.wait_ge(hid_done, 8 * rnd(f) + (k - 1))
                    else:
                        pe.wait_ge(dve_free, 8 * rnd(f) + (DVE_FREE0 + k - 9))
                    dst = mlp_tile(f, k)
                    for kt in range(8):
                        if j == 0 and kt % 2 == 0:
                            pe.wait_ge(w_lo, 16 * rnd(f) + (NU + 4 * g + kt // 2 + 1))
                        if k == 8:
                            pe.wait_ge(hid_lo, 8 * rnd(f) + (kt + 1))
                        w = ring(NU + 4 * g, kt)
                        if g < 2:
                            last = product(dst, tuple(x[:, j * P:(j + 1) * P] for x in w),
                                           (yhi[:, kt], ylo[:, kt]), kt, 7)
                        else:
                            last = product(dst, (hhi[:, kt, j * P:(j + 1) * P], hlo[:, kt, j * P:(j + 1) * P]),
                                           w, kt, 7)
                    last.then_inc(tile_done, 1)

            pe.wait_ge(*free_count(NS - 1))
            pe.wait_ge(*free_count(NS - 2))
            for half in range(2):
                pe.wait_ge(h_lo, 6 + 2 * half)
                tok = slice(256 * half, 256 * half + 256)
                for j in range(4):
                    for kt in range(8):
                        if half == 0 and j == 0 and kt % 2 == 0:
                            pe.wait_ge(w_lo, NU + kt // 2 + 1)
                        last = product(mlp_tile(0, j)[:, tok], tuple(x[:, j * P:(j + 1) * P] for x in ring(NU, kt)),
                                       (yhi[:, kt, tok], ylo[:, kt, tok]), kt, 7)
                    if half:
                        last.then_inc(tile_done, 1)
                if half == 0:
                    h2_tile(2)
                    h2_tile(3)

            with pe.Fori(0, NF - 1) as f:
                for g in (1, 2, 3):
                    mlp(f, g)
                mlp(f + 1, 0)
            for g in (1, 2, 3):
                mlp(LAST, g)


_INS = ["x", "ln_gains", "w_in", "conv_w", "conv_b", "rg_w_a", "rg_b_a", "rg_w_x", "rg_b_x", "rg_lambda",
        "lb_logits", "hgrn_norm", "w_branch", "w_out", "w_up", "w_down"]


def kernel(**inputs):
    import numpy as _np
    import concourse.bacc as _bacc
    from concourse import mybir as _mybir
    from concourse.bass_utils import run_bass_kernel_spmd as _run

    nc = _bacc.Bacc("TRN2", target_bir_lowering=False, num_devices=1, dynamic_dma_scratch_size=1024)
    arrays, args = {}, []
    for name in _INS:
        a = _np.ascontiguousarray(inputs[name])
        arrays[f"in_{name}"] = a
        args.append(nc.dram_tensor(f"in_{name}", a.shape, _mybir.dt.from_np(a.dtype), kind="ExternalInput").ap())
    shape = inputs["x"].shape
    args.append(nc.dram_tensor("out_x", shape, _mybir.dt.float32, kind="ExternalOutput").ap())
    trunk(nc, *args)
    r = _run(nc, [arrays], core_ids=[0])
    return r.results[0]["out_x"]
```

```python
from contextlib import ExitStack

import concourse.bass as bass
from concourse import mybir

F32 = mybir.dt.float32
F32R = mybir.dt.float32r
I8 = mybir.dt.int8
ALU = mybir.AluOpType
ACT = mybir.ActivationFunctionType

P = 128
RAW = 4
MRAW = 4
RING = 8
EPS = 1e-6
LB_FLOOR = 1e-30
RG_C = 8.0
EXP_LN_SET = "natural_log_exp_and_others"
SIGMOID_SET = "sigmoid_and_others"
SILU_SET = "silu_and_others"
SQRT_SET = "sqrt_and_others"

GROUPS = [
    ("tok", 6),
    ("feat", 0),
    ("feat", 4), ("feat", 5),
    ("feat", 2), ("feat", 1), ("tok", 3),
    ("feat", 8), ("br", (0, 0)), ("feat", 9), ("br", (0, 1)),
    ("feat", 10), ("feat", 11),
    ("tok", 7),
    ("br", (1, 0)), ("br", (1, 1)),
    ("feat", 12), ("feat", 13), ("br", (2, 0)), ("br", (2, 1)),
    ("out", 0), ("out", 1),
]
G_I, G_RG, G_Q, G_F, G_SK, G_SQ, G_SV = range(7)
G_GA = (7, 9)
G_GB = (11, 12)
G_G = 13
G_GC = (16, 17)
G_C = 18
G_OUT = (20, 21)
RG_AT = 4 * G_RG
NS = 4 * len(GROUPS)
UNITS = [2 if kind == "br" else 4 for kind, _ in GROUPS]
FIRST_UNIT = [sum(UNITS[:g]) for g in range(len(GROUPS) + 1)]
NU = FIRST_UNIT[-1]
OWNER = [g for g, n in enumerate(UNITS) for _ in range(n)]
BY_ACT = {G_I, G_SQ, G_SK, G_SV, *G_OUT}

HG_AT = [16 + 4 * h for h in range(4)]
LEVEL_AT = {(15 if (h, p) == (0, 0) else HG_AT[h] + p): (h, p)
            for h in range(4) for p in range(4)}
HG_OUT = [b + 5 for b in HG_AT]
ATT_Z = (33, 36, 38, 40, 43, 45, 47, 49)
ATT_S = (36, 38, 40, 43, 45, 47, 49, 51)
ON_AT = 52
YC_AT = 65
ATT_SP = [z + (GROUPS[(z + 1) // 4][0] == "br") for z in ATT_Z]
LEVELS = (32, 16, 8, 4, 2, 1)


def split_slots():
    at = [[] for _ in range(NS)]
    for g in range(1, len(GROUPS)):
        after_branch = UNITS[g] == 4 and UNITS[g - 1] == 2
        before = UNITS[g] == 2 and UNITS[g + 1] == 4 if g + 1 < len(GROUPS) else False
        for u in range(UNITS[g]):
            if after_branch:
                slot = 4 * (g - 2) + 2 + u if u < 2 else 4 * (g - 1)
            else:
                slot = 4 * (g - 1) + (u if before else u * 4 // UNITS[g])
            at[slot].append(FIRST_UNIT[g] + u)
    for u in range(4):
        at[NS - 4 + u].append(NU + u)
    return at


def trunk(nc, x, ln_gains, w_in, conv_w, conv_b, rg_w_a, rg_b_a, rg_w_x, rg_b_x,
          rg_lambda, lb_logits, hgrn_norm, w_branch, w_out, w_up, w_down, out):
    _, S, D = x.shape
    W = conv_b.shape[1]
    FF = w_up.shape[2]
    assert (S, D, W, FF) == (512, 1024, 512, 4096)
    NF = FF // 1024
    SPLIT_AT = split_slots()

    win_v = w_in[0].rearrange("(u two p) (b n) -> b u p two n", two=2, p=P, n=512)
    wbr_v = w_branch[0].rearrange("b (u two p) (h n) -> b h u p two n", two=2, p=P, n=512)
    wout_v = w_out[0].rearrange("(u two p) (h n) -> h u p two n", two=2, p=P, n=512)
    wup_v = w_up[0].rearrange("(u two p) (i q n) -> i q u p two n", two=2, p=P, q=2, n=512)
    wdn_v = w_down[0].rearrange("(i u two p) (h n) -> i h u p two n", two=2, p=P, u=4, n=512)
    x_v = x[0].rearrange("(t p) d -> t p d", p=P)
    out_v = out[0].rearrange("(t p) d -> t p d", p=P)

    def unit_source(U):
        g = OWNER[U]
        u = U - FIRST_UNIT[g]
        kind, what = GROUPS[g]
        if kind == "br":
            return wbr_v[what[0], what[1], u]
        return wout_v[what, u] if kind == "out" else win_v[what, u]

    with ExitStack() as ctx:
        def sb(name, shape, dt=F32):
            return ctx.enter_context(nc.sbuf_tensor(name, shape, dt))

        def sem(name):
            return ctx.enter_context(nc.semaphore(name))

        whi = sb("whi", [P, RING, 2, 512], F32R)
        wlo = sb("wlo", [P, RING, 2, 512], F32R)
        hhi = sb("hhi", [P, 8, 512], F32R)
        hlo = sb("hlo", [P, 8, 512], F32R)
        yhi = sb("yhi", [P, 8, 512], F32R)
        ylo = sb("ylo", [P, 8, 512], F32R)
        raw = sb("raw", [P, RAW, 2, 512])
        arena = sb("arena", [P, 18944])

        def at(col, *dims):
            n = 1
            for d in dims:
                n *= d
            ap = arena[:, col:col + n]
            if len(dims) == 2:
                ap = ap.rearrange("p (a b) -> p a b", b=dims[1])
            return ap

        scan_keep = sb("scan_keep", [P, 512])
        hgain = scan_keep[:, 0:P]
        key_sums = scan_keep[:, P:4 * P]

        XPW = 515
        rg_xp = at(0, 4, XPW)
        rg_xc = at(14336, 4, 512)
        rg_m = at(8192, 4, 512)
        rg_u = at(10240, 4, 512)
        rg_a = at(16896, 4, 512)
        rg_wa = at(16384, 4, 128)
        rg_wx = at(5632, 4, 128)
        hg_b = at(0, 4, 512)
        hg_k = at(2048, 4, 512)
        hg_q = at(4096, 4, 512)
        hg_v = at(6144, 4, 512)
        lev_q = [at(12288, 512), at(12800, 512)]
        lev_k = [at(13312, 512), at(13824, 512)]
        attn_t = at(14336, 4, 128)
        qb = at(14848, 512)
        f_t = [lev_q[0], lev_k[0], lev_q[0], qb]
        kdt = at(15360, 4, 128)
        states = at(15872, 7, 128)
        sb_v = at(16896, 4, 512)
        sb_q = at(8192, 4, 512)
        sb_k = at(10240, 4, 512)
        stick = [at(12288, 1280), at(13568, 1280)]
        merged = [at(512 * j, 512) for j in range(4)] + [at(14848 + 512 * j, 512) for j in range(4)]
        gates = [at(2048, 4, 512), at(4096, 4, 512), at(4096, 4, 512), at(2048, 4, 512),
                 at(4096, 4, 512), at(8192, 4, 512)]
        hg_g = at(10240, 4, 512)
        br_t = [at(12288, 512), at(13056, 512)]
        xin = at(0, 4, 1024)
        xn = [at(8192, 1024), at(9216, 1024)]
        xsq = at(10240, 1024)
        gain0 = at(11264, 1024)
        par_rows = at(12288, 128)
        x1 = at(0, 4, 1024)
        o4 = at(4096, 4, 1024)
        gain3 = at(8192, 1024)
        sq = at(9216, 1024)
        gain1 = at(10240, 1024)
        gain2 = at(11264, 1024)
        o_gain = at(16896, 512)
        relu = [at(10240, 512), at(10752, 512)]
        hid = [at(11264, 512), at(11776, 512)]
        mraw = arena[:, 12288:16384].rearrange("p (u two n) -> p u two n", u=MRAW, two=2)

        ident = sb("ident", [P, P])
        ntri = sb("ntri", [P, P])
        nones = sb("nones", [P, P])
        masks = sb("masks", [P, len(LEVELS), P], I8)
        NPAR = 36
        par = sb("par", [P, NPAR])
        c_conv = lambda k, j: par[:, 4 * k + j:4 * k + j + 1]
        c_convb, c_ba, c_bx, c_lam, c_lb = (par[:, 16 + 4 * i:20 + 4 * i] for i in range(5))
        chan = sb("chan", [P, 40])
        c8, c8n = chan[:, 0:4], chan[:, 4:8]
        ln1mlb, lnlb, ln_diff = chan[:, 8:12], chan[:, 12:16], chan[:, 16:20]
        ca, cb, cc = chan[:, 20:24], chan[:, 24:28], chan[:, 28:32]
        ss = sb("ss", [P, 4])
        ss_half, ms_half = chan[:, 32:36], chan[:, 36:40]
        rstd = sb("rstd", [P, 4])
        hg_ss = sb("hg_ss", [P, 16])
        hg_rstd = sb("hg_rstd", [P, 16])
        dec = sb("dec", [P, 8])
        epsb = sb("epsb", [P, 1])

        pmain = ctx.enter_context(nc.psum_tensor("pmain", [P, 2, 512], F32))
        pside = ctx.enter_context(nc.psum_tensor("pside", [P, 6, 512], F32))
        pz = pside[:, 0:3, :].rearrange("p a n -> p (a n)")
        pyb = pside[:, 3, :]
        ph = [pside[:, 4, :], pside[:, 5, :]]

        raw_in = [sem(f"raw_in{i}") for i in range(RAW)]
        mraw_in = [sem(f"mraw_in{i}") for i in range(MRAW)]
        x_in = [sem(f"x_in{i}") for i in range(4)]
        x_again = sem("x_again")
        par_in = sem("par_in")
        gain0_in = sem("gain0_in")
        rgw_in = sem("rgw_in")
        hgain_in = sem("hgain_in")
        gain1_in, gains_in = sem("gain1_in"), sem("gains_in")
        out_sent = sem("out_sent")
        w_hi, w_lo = sem("w_hi"), sem("w_lo")
        tile_done = sem("tile_done")
        act_free, dve_free = sem("act_free"), sem("dve_free")
        act_step, dve_step, pool_step = sem("act_step"), sem("dve_step"), sem("pool_step")
        const_ready = sem("const_ready")
        par_t = sem("par_t")
        par_ready = sem("par_ready")
        chan_a, chan_d = sem("chan_a"), sem("chan_d")
        rgw_zero = sem("rgw_zero")
        rms_done = sem("rms_done")
        mean_ready, half_sum, half_mean = sem("mean_ready"), sem("half_sum"), sem("half_mean")
        xn_ready, xn_t, h_hi, h_lo = sem("xn_ready"), sem("xn_t"), sem("h_hi"), sem("h_lo")
        rg_conv, rg_gate, rg_sig, rg_tanh, rg_exp, rg_ix = (
            sem(n) for n in ("rg_conv", "rg_gate", "rg_sig", "rg_tanh", "rg_exp", "rg_ix"))
        rg_mult2, rg_mult, rg_out, ya_hi, ya_lo = (
            sem(n) for n in ("rg_mult2", "rg_mult", "rg_out", "ya_hi", "ya_lo"))
        q_sig, f_ln, f_abs, f_lse, f_k, b_ready = (
            sem(n) for n in ("q_sig", "f_ln", "f_abs", "f_lse", "f_k", "b_ready"))
        lev_d, lev_e, lev_qe, lev_ke, lev_p, lev_m = (sem(f"lev_{n}") for n in ("d", "e", "qe", "ke", "p", "m"))
        kd_t, kd_ready, kv_done, st_ready, o_done, o_ready = (
            sem(n) for n in ("kd_t", "kd_ready", "kv_done", "st_ready", "o_done", "o_ready"))
        on_a, on_d, g_ready, oc_ready, oc_t, yc_hi, yc_lo = (
            sem(n) for n in ("on_a", "on_d", "g_ready", "oc_ready", "oc_t", "yc_hi", "yc_lo"))
        z_done, sp_ln, sp_ready, sp_masked, summed, suf_done, w_exp, w_ready, av_done, yb_hi, yb_lo = (
            sem(n) for n in ("z_done", "sp_ln", "sp_ready", "sp_masked", "summed", "suf_done", "w_exp", "w_ready",
                             "av_done", "yb_hi", "yb_lo"))
        gate_ready, merged_sum, merged_hi, merged_lo = (
            sem(n) for n in ("gate_ready", "merged_sum", "merged_hi", "merged_lo"))
        relu_done, hid_done, hid_hi, hid_lo = (sem(n) for n in ("relu_done", "hid_done", "hid_hi", "hid_lo"))
        sum_zero, y_done = sem("sum_zero"), sem("y_done")

        block = ctx.enter_context(nc.Block())

        def free_count(s):
            mine = (s // 4) in BY_ACT
            n = sum(1 for r in range(s + 1) if ((r // 4) in BY_ACT) == mine)
            return (act_free if mine else dve_free), n

        LAST = "last round"

        def rnd(f):
            return NF - 1 if f is LAST else f

        def mlp_tile(f, k):
            if type(f) is int and f == 0 and k in (2, 3):
                return pside[:, 4 + k - 2, :]
            return pmain[:, (NS + k) % 2]

        Z_AT = (0, 512, 1024, 896)
        DVE_FREE0 = sum(1 for r in range(NS) if (r // 4) not in BY_ACT)

        def halves(buf, m):
            v = buf.rearrange("p (b two m) -> p b two m", two=2, m=m)
            return v[:, :, 0, :], v[:, :, 1, :]

        @block.sync
        def _(sp):
            def load_unit(U):
                if U >= RAW:
                    sp.wait_ge(w_lo, U - RAW + 1)
                sp.dma_start(raw[:, U % RAW], unit_source(U)).then_inc(raw_in[U % RAW], 16)

            def load_x(t):
                sp.dma_start(xin[:, t], x_v[t]).then_inc(x_in[t], 16)

            load_x(0)
            sp.dma_start(gain0, ln_gains[0, 0:1, :].partition_broadcast(P)).then_inc(gain0_in, 16)
            for U in range(RAW):
                load_unit(U)
            for t in range(1, 4):
                load_x(t)
            sp.dma_start(par_rows[0:16], conv_w[0].rearrange("k (c p) -> (k c) p", p=P)).then_inc(par_in, 16)
            for i, v in enumerate((conv_b, rg_b_a, rg_b_x, rg_lambda, lb_logits)):
                sp.dma_start(par_rows[16 + 4 * i:20 + 4 * i],
                             v[0].rearrange("(c p) -> c p", p=P)).then_inc(par_in, 16)
            sp.wait_ge(rgw_zero, 1)
            for w, dst in ((rg_w_a, rg_wa), (rg_w_x, rg_wx)):
                for half in range(2):
                    src = w[0].rearrange("(j two) c d -> two c j d", two=2)[half]
                    sp.dma_start(dst[64 * half:64 * half + 64, :, 64 * half:64 * half + 64],
                                 src).then_inc(rgw_in, 16)
            for U in range(RAW, NU):
                if U == FIRST_UNIT[G_GB[0]]:
                    sp.wait_ge(b_ready, 4)
                    sp.dma_start(hgain, hgrn_norm[0:1, :].partition_broadcast(P)).then_inc(hgain_in, 16)
                load_unit(U)
            sp.wait_ge(merged_lo, 8)
            sp.dma_start(gain1, ln_gains[0, 1:2, :].partition_broadcast(P)).then_inc(gain1_in, 16)
            for t in range(4):
                sp.dma_start(x1[:, t], x_v[t]).then_inc(x_again, 16)
            for i, g in ((2, gain2), (3, gain3)):
                sp.dma_start(g, ln_gains[0, i:i + 1, :].partition_broadcast(P)).then_inc(gains_in, 16)

            with sp.Fori(0, NF) as f:
                for g in range(4):
                    for u in range(4):
                        n = 4 * g + u
                        sp.wait_ge(w_lo, 16 * f + (NU + n - MRAW + 1))
                        src = wup_v[f, g, u] if g < 2 else wdn_v[f, g - 2, u]
                        sp.dma_start(mraw[:, n % MRAW], src).then_inc(mraw_in[n % MRAW], 16)
            for t in range(4):
                for half in range(2):
                    c = slice(512 * half, 512 * half + 512)
                    sp.wait_ge(y_done, 2 * t + half + 1)
                    sp.dma_start(out_v[t][:, c], o4[:, t, c]).then_inc(out_sent, 16)
            sp.wait_ge(out_sent, 128)

        @block.gpsimd
        def _(pool):
            count = [0]

            def step(ins):
                count[0] += 1
                ins.then_inc(pool_step, 1)
                pool.wait_ge(pool_step, count[0])

            g = nc.gpsimd
            g.memset(epsb[:], EPS)
            step(g.memset(ident[:], 0.0))
            step(g.affine_select(out=ident[:], in_=ident[:], compare_op=ALU.not_equal, fill=1.0, base=0,
                                 pattern=[[-1, P]], channel_multiplier=1))
            g.memset(nones[:], -1.0).then_inc(const_ready, 1)
            step(g.memset(ntri[:], -1.0))
            step(g.affine_select(out=ntri[:], in_=ntri[:], compare_op=ALU.is_ge, fill=0.0, base=0,
                                 pattern=[[-1, P]], channel_multiplier=1))
            step(g.memset(scan_keep[:], 1.0))
            g.memset(scan_keep[:].rearrange("p (c n) -> p c n", n=64)[:, :, 0:1], 0.0).then_inc(const_ready, 1)
            g.memset(lev_k[1], 0.0)
            g.memset(rg_wa, 0.0)
            g.memset(rg_wx, 0.0).then_inc(rgw_zero, 1)
            step(g.memset(masks[:], 0))
            for l, m in enumerate(LEVELS):
                second = masks[:, l, :].rearrange("p (b two m) -> p b two m", two=2, m=m)[:, :, 1, :]
                nb = P // (2 * m)
                step(g.memset(second, 1))
                step(g.affine_select(out=second, in_=second, compare_op=ALU.is_ge, fill=0.0, base=0,
                                     pattern=[[-2 * m, nb], [0, m]], channel_multiplier=1))
                last = g.affine_select(out=second, in_=second, compare_op=ALU.is_ge, fill=0.0, base=m - 1,
                                       pattern=[[2 * m, nb], [0, m]], channel_multiplier=-1)
                if l < len(LEVELS) - 1:
                    step(last)
            last.then_inc(const_ready, 1)

            def level_k(h, p):
                if p == 0:
                    pool.wait_ge(f_k, h + 1)
                if h == 0 and p == 1:
                    pool.wait_ge(b_ready, 2)
                for i in range(2):
                    r = 2 * p + i
                    if r == 0:
                        continue
                    pool.wait_ge(lev_e, 7 * h + r)
                    if r >= 3:
                        pool.wait_ge(lev_p, 7 * h + r - 1)
                    elif h:
                        pool.wait_ge(lev_p, 7 * h)
                        pool.wait_ge(kd_t, h)
                    if r == 7:
                        g.tensor_tensor(lev_k[i], hg_k[:, h], lev_q[i], ALU.mult).then_inc(lev_ke, 1)
                    else:
                        first = [halves(b, LEVELS[r - 1])[0] for b in (lev_k[i], hg_k[:, h], lev_q[i])]
                        g.tensor_tensor(*first, ALU.mult).then_inc(lev_ke, 1)

            def causal(buf, done):
                diag = buf[:, 0:1152].rearrange("p (b n) -> p b n", n=128)[:, 0:9:4, :]
                g.affine_select(out=diag, in_=diag, compare_op=ALU.is_gt, fill=0.0, base=0,
                                pattern=[[0, 3], [1, P]], channel_multiplier=-1)
                g.affine_select(out=buf[:, 896:1024], in_=buf[:, 896:1024], compare_op=ALU.is_gt, fill=0.0,
                                base=0, pattern=[[1, P]], channel_multiplier=-1).then_inc(done, 1)

            def sum_keys(a):
                sp_ = stick[a % 2]
                s12, s123, s23 = (key_sums[:, P * i:P * i + P] for i in range(3))
                pool.wait_ge(sp_masked, a + 1)

                def block(b, t):
                    return sp_[:, Z_AT[b] + P * (t - b):Z_AT[b] + P * (t - b) + P]

                g.tensor_tensor(s12, block(1, 2), block(2, 2), ALU.add)
                step(g.tensor_tensor(s23, block(2, 3), block(3, 3), ALU.add))
                g.tensor_tensor(s123, block(1, 3), s23, ALU.add).then_inc(summed, 1)

            for s in range(NS):
                kind, what = GROUPS[s // 4]
                if kind == "br" and what[0]:
                    d = 4 * what[1] + s % 4
                    pool.wait_ge(*free_count(s))
                    g.tensor_tensor(merged[d], merged[d], br_t[d % 2], ALU.add).then_inc(merged_sum, 1)
                if RG_AT + 2 <= s < RG_AT + 6:
                    j = s - RG_AT - 2
                    pool.wait_ge(rg_sig, 2 * j + 2)
                    g.tensor_tensor(rg_u[:, j], rg_u[:, j], rg_xc[:, j], ALU.mult).then_inc(rg_ix, 1)
                if s in LEVEL_AT:
                    level_k(*LEVEL_AT[s])
                for a in range(8):
                    if s == ATT_S[a]:
                        pool.wait_ge(w_exp, a + 1)
                        causal(stick[a % 2], w_ready)
                for a in range(8):
                    if s == ATT_Z[a]:
                        pool.wait_ge(sp_ready, a + 1)
                        if a == 0:
                            pool.wait_ge(b_ready, 4)
                        causal(stick[a % 2], sp_masked)
                        sum_keys(a)

            pool.wait_ge(xn_t, 8)
            g.memset(o4, 0.0).then_inc(sum_zero, 1)

        @block.scalar
        def _(act):
            a_ = nc.scalar
            n = {}

            def mark(ins, s):
                n[s.name] = n.get(s.name, 0) + 1
                ins.then_inc(s, 1)
                n["last"] = (s, n[s.name])

            def after():
                act.wait_ge(*n["last"])

            def step(ins):
                mark(ins, act_step)

            def split_hi(U):
                act.wait_ge(raw_in[U % RAW], 16 * (U // RAW + 1))
                if U >= RING:
                    act.wait_ge(tile_done, 4 * (OWNER[U - RING] + 1))
                mark(a_.activation(whi[:, U % RING], raw[:, U % RAW], ACT.Copy), w_hi)

            def split_hi_mlp(f, u):
                act.wait_ge(mraw_in[u % MRAW], 64 * f + 16 * (u // MRAW + 1))
                act.wait_ge(tile_done, 16 * f + (NS + 4 * (u // 4) - 4))
                a_.activation(whi[:, (NU + u) % RING], mraw[:, u % MRAW], ACT.Copy).then_inc(w_hi, 1)

            loaded = [None]

            def tables(name):
                if loaded[0] != name:
                    a_.preload_act_table_set(name)
                    loaded[0] = name

            def mean_root(t, rest=None):
                mark(a_.activation(ss[:, t:t + 1], ss[:, t:t + 1], ACT.Sqrt, scale=1.0 / D,
                                   bias=epsb[:] if rest is None else rest), rms_done)

            def round_t(dst, t, bank):
                src = pside[:, bank:bank + 2, :].rearrange("p a (b n) -> p (a b) n", n=P)
                mark(a_.activation(dst[:, :, t * P:(t + 1) * P], src, ACT.Copy), h_hi)

            def second_mean(t):
                act.wait_ge(mean_ready, t + 1)
                step(a_.activation(sq, x1[:, t], ACT.Square, accum_out=ss[:, t:t + 1]))
                after()
                mean_root(t)

            tables(SQRT_SET)
            act.wait_ge(const_ready, 1)
            def first_mean(t):
                act.wait_ge(x_in[t], 16)
                step(a_.activation(xsq, xin[:, t], ACT.Square, accum_out=ss[:, t:t + 1]))
                after()
                mean_root(t)

            def first_round(t):
                act.wait_ge(xn_t, t + 1)
                round_t(hhi, t, 2 * (t % 2))

            first_mean(0)
            split_hi(0)
            first_round(0)
            split_hi(1)
            split_hi(2)
            split_hi(3)
            first_mean(1)
            first_mean(2)
            first_round(1)

            def channel_constants():
                act.wait_ge(par_ready, 1)
                tables(EXP_LN_SET)
                step(a_.activation(ca, c_lam, ACT.Abs))
                after()
                step(a_.activation(ca, ca, ACT.Exp, scale=-1.0))
                after()
                mark(a_.activation(ca, ca, ACT.Ln, bias=1.0), chan_a)
                act.wait_ge(chan_d, 2)
                mark(a_.activation(ln1mlb, cb, ACT.Ln, bias=1.0, scale=-1.0), chan_a)
                act.wait_ge(chan_d, 3)
                mark(a_.activation(lnlb, cc, ACT.Ln), chan_a)

            def rg_sigmoids(j):
                tables(SIGMOID_SET)
                act.wait_ge(rg_gate, j + 1)
                mark(a_.activation(rg_a[:, j], ph[0], ACT.Sigmoid, bias=c_ba[:, j:j + 1]), rg_sig)
                r_there = n["last"]
                mark(a_.activation(rg_u[:, j], ph[1], ACT.Sigmoid, bias=c_bx[:, j:j + 1]), rg_sig)
                if j == 0:
                    act.wait_ge(chan_d, 1)
                act.wait_ge(*r_there)
                mark(a_.activation(rg_m[:, j], rg_a[:, j], ACT.Tanh, scale=c8n[:, j:j + 1]), rg_tanh)

            def forget_gate(first, second):
                tables(EXP_LN_SET)
                if first is not None:
                    a = f_t[first]
                    act.wait_ge(tile_done, 4 * G_F + first + 1)
                    if first >= 2:
                        act.wait_ge(b_ready, first - 1)
                    step(a_.activation(a, pmain[:, first % 2], ACT.Abs))
                    a_there = n["last"]
                if second is not None:
                    b = f_t[second]
                    act.wait_ge(*free_count(4 * G_F + second))
                    mark(a_.activation(b, hg_b[:, second], ACT.Abs, bias=ln_diff[:, second:second + 1]), f_abs)
                    b_there = n["last"]
                if first is not None:
                    act.wait_ge(*a_there)
                    step(a_.activation(a, a, ACT.Exp, scale=-1.0))
                    a_there = n["last"]
                if second is not None:
                    act.wait_ge(*b_there)
                    step(a_.activation(b, b, ACT.Exp, scale=-1.0))
                    b_there = n["last"]
                if first is not None:
                    act.wait_ge(*a_there)
                    mark(a_.activation(a, a, ACT.Ln, bias=1.0), f_ln)
                if second is not None:
                    act.wait_ge(*b_there)
                    mark(a_.activation(b, b, ACT.Ln, bias=1.0), f_lse)
                    mark(a_.activation(hg_k[:, second], hg_k[:, second], ACT.Exp, scale=-1.0,
                                       bias=ln1mlb[:, second:second + 1]), f_k)

            def level_exp(h, p):
                for i in range(2):
                    r = 2 * p + i
                    if r == 0:
                        continue
                    act.wait_ge(lev_d, 7 * h + r)
                    if r == 7:
                        mark(a_.activation(lev_q[i], lev_q[i], ACT.Exp, scale=-1.0), lev_e)
                    else:
                        first, second = halves(lev_q[i], LEVELS[r - 1])
                        a_.activation(first, first, ACT.Exp, scale=-1.0)
                        mark(a_.activation(second, second, ACT.Exp), lev_e)
                if p == 3:
                    if h:
                        act.wait_ge(o_done, h)
                        act.wait_ge(st_ready, 7 * h)
                    step(a_.activation(dec[:], hg_b[:, h].rearrange("p (c n) -> p c n", n=64)[:, :, 63], ACT.Exp))
                    mark(a_.activation(qb, hg_b[:, h], ACT.Exp), kd_ready)

            for s in range(NS):
                g, j = divmod(s, 4)
                if s == 0:
                    first_mean(3)
                for U in SPLIT_AT[s]:
                    if U < NU:
                        split_hi(U)
                    else:
                        split_hi_mlp(0, U - NU)
                d = s - 4 * G_C - 1
                if 0 <= d < 8:
                    act.wait_ge(merged_sum, 8 + d + 1)
                    mark(a_.activation(hhi[:, d], merged[d], ACT.Copy), merged_hi)

                if s in LEVEL_AT:
                    level_exp(*LEVEL_AT[s])
                if s == 4 * G_F + 4:
                    forget_gate(None, 3)
                if s == 4 * G_F + 5:
                    act.wait_ge(rg_out, 4)
                    mark(a_.activation(yhi[:, 0:4], rg_m, ACT.Copy), ya_hi)
                ps = pmain[:, s % 2]
                if g in BY_ACT and g not in G_OUT or g == G_Q:
                    act.wait_ge(tile_done, s + 1)
                if g == G_Q:
                    tables(SIGMOID_SET)
                    mark(a_.activation(hg_q[:, j], ps, ACT.Sigmoid), q_sig)
                if RG_AT + 2 <= s < RG_AT + 6:
                    rg_sigmoids(s - RG_AT - 2)
                if s == RG_AT + 5:
                    tables(EXP_LN_SET)
                    act.wait_ge(rg_tanh, 4)
                    for j4 in range(4):
                        mark(a_.activation(rg_a[:, j4], rg_a[:, j4], ACT.Exp, scale=c8[:, j4:j4 + 1]), rg_exp)
                    after()
                    act.wait_ge(rg_ix, 4)
                    mark(a_.activation(rg_xc, rg_a, ACT.Square), rg_exp)
                if g == G_F:
                    forget_gate(j, j - 1 if j else None)
                if g == G_I:
                    mark(a_.activation(hg_v[:, j], ps, ACT.Copy), act_free)
                    if j < 2:
                        first_round(j + 2)
                    if j == 3:
                        channel_constants()
                if g == G_SQ:
                    act.wait_ge(ya_lo, 1)
                    mark(a_.activation(sb_q[:, j], ps, ACT.Copy, scale=0.125), act_free)
                if g == G_SK:
                    mark(a_.activation(sb_k[:, j], ps, ACT.Copy), act_free)
                if g == G_SV:
                    mark(a_.activation(sb_v[:, j], ps, ACT.Copy), act_free)

                if s == RG_AT + 7:
                    tables(SQRT_SET)
                    act.wait_ge(rg_mult2, 2)
                    mark(a_.activation(rg_m, rg_m, ACT.Sqrt), rg_mult)

                for h, b in enumerate(HG_AT):
                    if s == b + 3:
                        act.wait_ge(kd_t, h + 1)
                        if h:
                            act.wait_ge(kv_done, h)
                        mark(a_.activation(kdt, pside[:, 0, :].rearrange("p (a b) -> p a b", b=P), ACT.Copy), kd_ready)

                for a in range(8):
                    if s == ATT_S[a]:
                        tables(EXP_LN_SET)
                        act.wait_ge(suf_done, a + 1)
                        mark(a_.activation(stick[a % 2], pz[:, 0:1280], ACT.Exp), w_exp)
                for k, gg in enumerate((*G_GA, *G_GB, *G_GC)):
                    last = 4 * gg + 3
                    if s == last + (k in (1, 2)):
                        tables(SIGMOID_SET)
                        act.wait_ge(dve_free, free_count(last)[1])
                        buf = gates[k]
                        mark(a_.activation(buf, buf, ACT.Sigmoid), gate_ready)
                for a in range(8):
                    if s == ATT_Z[a]:
                        buf = stick[a % 2]
                        tables(EXP_LN_SET)
                        act.wait_ge(z_done, a + 1)
                        if a >= 2:
                            act.wait_ge(av_done, a - 1)
                        elif a == 0:
                            act.wait_ge(lev_p, 28)
                            act.wait_ge(kd_t, 4)
                        else:
                            act.wait_ge(o_done, 4)
                        step(a_.activation(buf, pz[:, 0:1280], ACT.Abs))
                        after()
                        step(a_.activation(buf, buf, ACT.Exp, scale=-1.0))
                        after()
                        mark(a_.activation(buf, buf, ACT.Ln, bias=1.0), sp_ln)
                for a in range(1, 8, 2):
                    if s == ATT_S[a]:
                        act.wait_ge(av_done, a + 1)
                        mark(a_.activation(yhi[:, 4 + a // 2], pyb, ACT.Copy), yb_hi)

                if s == 4 * G_G + 3:
                    tables(SILU_SET)
                    act.wait_ge(dve_free, free_count(s)[1])
                    mark(a_.activation(hg_g, hg_g, ACT.Silu), g_ready)

                if s == ON_AT:
                    act.wait_ge(o_ready, 4)
                    for i in range(16):
                        t, h = divmod(i, 4)
                        if i == 8:
                            after()
                        step(a_.activation(ph[i // 4 % 2][:, h * P:(h + 1) * P], hg_v[:, t, h * P:(h + 1) * P],
                                           ACT.Square, accum_out=hg_ss[:, i:i + 1]))
                    after()
                    tables(SQRT_SET)
                    mark(a_.activation(hg_ss[:], hg_ss[:], ACT.Sqrt, bias=epsb[:], scale=1.0 / P), on_a)
                for t in range(4):
                    if s == YC_AT + t:
                        act.wait_ge(oc_t, t + 1)
                        mark(a_.activation(yhi[:, 0:4, t * P:(t + 1) * P],
                                           pside[:, t % 2].rearrange("p (a b) -> p a b", b=P), ACT.Copy), yc_hi)

                if g in G_OUT:
                    half = g - G_OUT[0]
                    if half == 0 and j == 0:
                        act.wait_ge(merged_lo, 8)
                        tables(SQRT_SET)
                    if half and j >= 2:
                        act.wait_ge(xn_t, 4 + j - 1)
                        round_t(yhi, j - 2, 2 * (j % 2))
                    act.wait_ge(tile_done, s + 1)
                    part = o4[:, j, 512 * half:512 * half + 512]
                    mark(a_.activation(part, ps, ACT.Copy), act_free)
                    after()
                    if half == 0:
                        mark(a_.activation(sq[:, 0:512], part, ACT.Square, accum_out=ss_half[:, j:j + 1]), half_sum)
                        after()
                    else:
                        step(a_.activation(sq[:, 0:512], part, ACT.Square, accum_out=ss[:, j:j + 1]))
                        after()
                        act.wait_ge(half_mean, j + 1)
                        mean_root(j, ms_half[:, j:j + 1])
                        if j < 2:
                            second_mean(j)

            second_mean(2)
            second_mean(3)
            for t in (2, 3):
                act.wait_ge(xn_t, 4 + t + 1)
                round_t(yhi, t, 2 * (t % 2))

            def mlp(f, g):
                for j in range(4):
                    k = 4 * g + j
                    if f is not LAST or g < 3:
                        split_hi_mlp(rnd(f), k + 4)
                    act.wait_ge(tile_done, 16 * rnd(f) + (NS + k + 1))
                    if g < 2:
                        if k >= 2:
                            act.wait_ge(hid_done, 8 * rnd(f) + (k - 1))
                        a_.activation(relu[k % 2], mlp_tile(f, k), ACT.Relu).then_inc(relu_done, 1)
                        act.wait_ge(hid_done, 8 * rnd(f) + (k + 1))
                        a_.activation(hhi[:, k], hid[k % 2], ACT.Copy).then_inc(hid_hi, 1)
                    elif f is LAST:
                        half = g - 2
                        act.wait_ge(dve_free, DVE_FREE0 + 8 * (NF - 1) + 4 * half + j + 1)
                        part = o4[:, j, 512 * half:512 * half + 512]
                        if half == 0:
                            mark(a_.activation(sq[:, 0:512], part, ACT.Square, accum_out=ss_half[:, j:j + 1]), half_sum)
                            after()
                        else:
                            step(a_.activation(sq[:, 0:512], part, ACT.Square, accum_out=ss[:, j:j + 1]))
                            after()
                            act.wait_ge(half_mean, 4 + j + 1)
                            mean_root(j, ms_half[:, j:j + 1])

            mlp(0, 0)
            with act.Fori(0, NF - 1) as f:
                for g in (1, 2, 3):
                    mlp(f, g)
                mlp(f + 1, 0)
            for g in (1, 2, 3):
                mlp(LAST, g)

        @block.vector
        def _(dve):
            v = nc.vector
            n = {}

            def mark(ins, s):
                n[s.name] = n.get(s.name, 0) + 1
                ins.then_inc(s, 1)
                n["last"] = (s, n[s.name])

            def after():
                dve.wait_ge(*n["last"])

            def step(ins):
                mark(ins, dve_step)

            def split_lo(U):
                dve.wait_ge(w_hi, U + 1)
                mark(v.tensor_tensor(wlo[:, U % RING], raw[:, U % RAW], whi[:, U % RING].bitcast(F32), ALU.subtract), w_lo)

            def split_lo_mlp(f, u):
                dve.wait_ge(w_hi, 16 * f + (NU + u + 1))
                v.tensor_tensor(wlo[:, (NU + u) % RING], mraw[:, u % MRAW],
                                whi[:, (NU + u) % RING].bitcast(F32), ALU.subtract).then_inc(w_lo, 1)

            def take(dst, s):
                dve.wait_ge(tile_done, s + 1)
                mark(v.tensor_copy(dst, pmain[:, s % 2]), dve_free)

            def half_to_mean(t, n_sums):
                dve.wait_ge(half_sum, n_sums)
                mark(v.tensor_scalar(ms_half[:, t:t + 1], ss_half[:, t:t + 1], 1.0 / D, EPS, ALU.mult, ALU.add), half_mean)

            def norm_scale(dst, src, t, gain, done):
                step(v.reciprocal(rstd[:, t:t + 1], ss[:, t:t + 1]))
                after()
                mark(v.scalar_tensor_tensor(dst, src, rstd[:, t:t + 1], gain, ALU.mult, ALU.mult), done)

            def rest_t(hi, lo, t, bank):
                src = pside[:, bank:bank + 2, :].rearrange("p a (b n) -> p (a b) n", n=P)
                mark(v.tensor_tensor(lo[:, :, t * P:(t + 1) * P], src, hi[:, :, t * P:(t + 1) * P].bitcast(F32),
                                     ALU.subtract), h_lo)

            def first_scale(t):
                dve.wait_ge(rms_done, t + 1)
                if t >= 2:
                    dve.wait_ge(xn_t, t - 1)
                norm_scale(xn[t % 2], xin[:, t], t, gain0, xn_ready)

            def first_rest(t):
                dve.wait_ge(h_hi, t + 1)
                rest_t(hhi, hlo, t, 2 * (t % 2))

            dve.wait_ge(gain0_in, 16)
            first_scale(0)
            split_lo(0)
            first_rest(0)
            split_lo(1)
            split_lo(2)
            split_lo(3)
            first_scale(1)
            first_scale(2)
            first_rest(1)

            def channel_constants():
                dve.wait_ge(par_t, 1)
                mark(v.tensor_copy(par[:], ph[0][:, 0:NPAR]), par_ready)
                after()
                dve.wait_ge(chan_a, 1)
                step(v.tensor_scalar(cb, c_lam, 0.0, None, ALU.min))
                after()
                step(v.tensor_tensor(ca, ca, cb, ALU.subtract))
                after()
                step(v.tensor_scalar(c8n, ca, RG_C, None, ALU.mult))
                mark(v.tensor_scalar(c8, ca, -RG_C, None, ALU.mult), chan_d)
                after()
                step(v.tensor_tensor(cb, c_lb, c_lb, ALU.subtract))
                after()
                step(v.tensor_scalar(cc, cb, 1.0, None, ALU.add))
                after()
                mark(v.tensor_tensor(cb, cc, cc, ALU.subtract), chan_d)
                after()
                mark(v.tensor_scalar(cc, cb, LB_FLOOR, 2.0 ** 50, ALU.max, ALU.mult), chan_d)
                dve.wait_ge(chan_a, 3)
                mark(v.tensor_scalar(lnlb, lnlb, -50.0 * 0.6931471805599453, None, ALU.add), chan_d)
                after()
                mark(v.tensor_tensor(ln_diff, ln1mlb, lnlb, ALU.subtract), chan_d)
                step(v.memset(rg_xp[:, :, 0:3], 0.0))
                after()

            def forget_gate_first(h):
                ps = pmain[:, h % 2]
                dve.wait_ge(f_ln, h + 1)
                step(v.scalar_tensor_tensor(hg_b[:, h], ps, 0.0, f_t[h], ALU.min, ALU.subtract))
                mark(v.scalar_tensor_tensor(hg_k[:, h], ps, 0.0, f_t[h], ALU.max, ALU.add), dve_free)

            def forget_gate_second(h):
                dve.wait_ge(f_abs, h + 1)
                step(v.tensor_scalar(hg_b[:, h], hg_b[:, h], ln1mlb[:, h:h + 1], lnlb[:, h:h + 1], ALU.add, ALU.max))
                after()
                dve.wait_ge(f_lse, h + 1)
                step(v.tensor_tensor(f_t[h], f_t[h], hg_b[:, h], ALU.add))
                after()
                mark(v.tensor_tensor_scan(hg_b[:, h], scan_keep[:], f_t[h], 0.0, ALU.mult, ALU.add), b_ready)

            def level_exponents(h, p):
                for i in range(2):
                    r = 2 * p + i
                    if r == 0:
                        continue
                    if 8 * h + r >= 2:
                        prev = 8 * h + r - 2
                        if prev % 8:
                            dve.wait_ge(lev_ke, 7 * (prev // 8) + prev % 8)
                        if prev % 8 not in (0, 7):
                            dve.wait_ge(lev_p, 7 * (prev // 8) + prev % 8 + 1)
                    if r == 7:
                        b64 = hg_b[:, h].rearrange("p (c n) -> p c n", n=64)
                        mark(v.tensor_tensor(lev_q[i].rearrange("p (c n) -> p c n", n=64), b64,
                                             b64[:, :, 63:64].to_broadcast((P, 8, 64)), ALU.subtract), lev_d)
                    else:
                        m = LEVELS[r - 1]
                        bb = hg_b[:, h].rearrange("p (c n) -> p c n", n=2 * m)
                        mark(v.tensor_tensor(lev_q[i].rearrange("p (c n) -> p c n", n=2 * m), bb,
                                             bb[:, :, m - 1:m].to_broadcast((P, S // (2 * m), 2 * m)),
                                             ALU.subtract), lev_d)

            def level_q(h, p):
                for i in range(2):
                    r = 2 * p + i
                    if r in (0, 7):
                        continue
                    dve.wait_ge(lev_e, 7 * h + r)
                    dst = halves(lev_q[i], LEVELS[r - 1])[1]
                    mark(v.tensor_tensor(dst, halves(hg_q[:, h], LEVELS[r - 1])[1], dst, ALU.mult), lev_qe)
                if p == 3:
                    dve.wait_ge(kd_ready, 2 * h + 1)
                    mark(v.tensor_tensor(qb, hg_q[:, h], qb, ALU.mult), lev_qe)

            def merged_rest(d):
                dve.wait_ge(merged_hi, d + 1)
                mark(v.tensor_tensor(hlo[:, d], merged[d], hhi[:, d].bitcast(F32), ALU.subtract), merged_lo)

            def level_merge(h, p):
                for i in range(2):
                    r = 2 * p + i
                    if r == 7:
                        continue
                    dve.wait_ge(lev_p, 7 * h + r + 1)
                    ps = ph[i].rearrange("p (a b) -> p a b", b=P)
                    if r == 0:
                        if h:
                            dve.wait_ge(kv_done, h)
                        mark(v.tensor_tensor(attn_t, ps, ident[:].unsqueeze(1).to_broadcast((P, 4, P)), ALU.mult), lev_m)
                    else:
                        after()
                        second = [b.rearrange("p t (b two m) -> p t b two m", two=2, m=LEVELS[r - 1])[:, :, :, 1, :]
                                  for b in (attn_t, masks[:, r - 1:r], ps)]
                        second[1] = second[1].to_broadcast((P, 4, P // (2 * LEVELS[r - 1]), LEVELS[r - 1]))
                        mark(v.copy_predicated(*second), lev_m)

            def chunk_states(h):
                dve.wait_ge(kv_done, h + 1)
                if h:
                    dve.wait_ge(o_done, h)
                for c in range(7):
                    kv = pside[:, 1 + c % 2, (c // 2) * P:(c // 2 + 1) * P]
                    if c == 0:
                        mark(v.tensor_copy(states[:, 0], kv), st_ready)
                    else:
                        after()
                        mark(v.scalar_tensor_tensor(states[:, c], states[:, c - 1], dec[:, c:c + 1], kv,
                                                    ALU.mult, ALU.add), st_ready)

            def first_norm(t, n_means):
                dve.wait_ge(act_free, free_count(4 * G_OUT[1] + t)[1])
                step(v.tensor_tensor(o_gain, o4[:, t, 512:1024], gain1[:, 512:1024], ALU.mult))
                if t == 2:
                    dve.wait_ge(h_hi, 6)
                    rest_t(yhi, ylo, 1, 2)
                dve.wait_ge(rms_done, n_means)
                step(v.reciprocal(rstd[:, t:t + 1], ss[:, t:t + 1]))
                after()
                step(v.scalar_tensor_tensor(x1[:, t, 0:512], o4[:, t, 0:512], rstd[:, t:t + 1], x1[:, t, 0:512],
                                            ALU.mult, ALU.add))
                mark(v.scalar_tensor_tensor(x1[:, t, 512:1024], o_gain, rstd[:, t:t + 1], x1[:, t, 512:1024],
                                            ALU.mult, ALU.add), mean_ready)
                after()
                step(v.tensor_tensor(o4[:, t], x1[:, t], gain2, ALU.mult))

            def second_norm(t, n_means):
                dve.wait_ge(rms_done, n_means)
                step(v.reciprocal(rstd[:, t:t + 1], ss[:, t:t + 1]))
                after()
                mark(v.tensor_scalar(o4[:, t], o4[:, t], rstd[:, t:t + 1], None, ALU.mult), xn_ready)

            for s in range(NS):
                g, j = divmod(s, 4)
                if s == 0:
                    first_scale(3)
                if s in LEVEL_AT:
                    if LEVEL_AT[s] == (0, 0):
                        dve.wait_ge(*free_count(4 * G_Q + 3))
                        dve.wait_ge(const_ready, 3)
                        dve.wait_ge(b_ready, 1)
                    if LEVEL_AT[s] == (0, 1):
                        dve.wait_ge(b_ready, 3)
                    level_exponents(*LEVEL_AT[s])
                if s == HG_AT[3] + 4:
                    chunk_states(3)
                for U in SPLIT_AT[s]:
                    split_lo(U) if U < NU else split_lo_mlp(0, U - NU)
                if s in LEVEL_AT:
                    level_q(*LEVEL_AT[s])
                if s == 4 * G_F + 5:
                    forget_gate_second(3)

                ps = pmain[:, s % 2]
                if s < 2:
                    first_rest(s + 2)
                if s == 3:
                    channel_constants()
                if g == G_RG:
                    take(rg_xp[:, j, 3:XPW], s)
                    after()
                    step(v.tensor_scalar(rg_xc[:, j], rg_xp[:, j, 0:512], c_conv(0, j), c_convb[:, j:j + 1],
                                         ALU.mult, ALU.add))
                    for k in range(1, 4):
                        after()
                        ins = v.scalar_tensor_tensor(rg_xc[:, j], rg_xp[:, j, k:k + 512], c_conv(k, j), rg_xc[:, j],
                                                     ALU.mult, ALU.add)
                        mark(ins, rg_conv) if k == 3 else step(ins)
                if g == G_Q:
                    dve.wait_ge(q_sig, j + 1)
                    mark(v.tensor_tensor(hg_q[:, j], ps, hg_q[:, j], ALU.mult), dve_free)
                if g == G_F:
                    if j == 0:
                        dve.wait_ge(const_ready, 2)
                    forget_gate_first(j)
                    if j:
                        forget_gate_second(j - 1)
                if s == RG_AT + 6:
                    dve.wait_ge(rg_exp, 5)
                    mark(v.scalar_tensor_tensor(rg_m, rg_xc, 1.0, rg_m, ALU.add, ALU.mult), rg_mult2)
                    after()
                    mark(v.tensor_scalar(rg_m, rg_m, 0.0, None, ALU.max), rg_mult2)
                if s == RG_AT + 8:
                    dve.wait_ge(rg_mult, 1)
                    step(v.memset(rg_m[:, :, 0:1], 1.0))
                    after()
                    step(v.tensor_tensor(rg_u, rg_u, rg_m, ALU.mult))
                    after()
                if s == RG_AT + 9:
                    for j4 in range(4):
                        mark(v.tensor_tensor_scan(rg_m[:, j4], rg_a[:, j4], rg_u[:, j4], 0.0,
                                                  ALU.mult, ALU.add), rg_out)

                if s == RG_AT + 14:
                    dve.wait_ge(ya_hi, 1)
                    mark(v.tensor_tensor(ylo[:, 0:4], rg_m, yhi[:, 0:4].bitcast(F32), ALU.subtract), ya_lo)
                for h, b in enumerate(HG_AT):
                    if b <= s < b + 4:
                        level_merge(h, s - b)
                    if s == b + 4 and h < 3:
                        chunk_states(h)
                    if s == HG_OUT[h]:
                        dve.wait_ge(o_done, h + 1)
                        mark(v.tensor_copy(hg_v[:, :, h * P:(h + 1) * P], pyb.rearrange("p (a b) -> p a b", b=P)), o_ready)

                for k, gg in enumerate((*G_GA, *G_GB, *G_GC)):
                    if g == gg:
                        if gg == G_GA[0] and j in (0, 3):
                            dve.wait_ge(lev_ke, 21 if j == 0 else 28)
                        if gg == G_GC[1] and j == 0:
                            dve.wait_ge(z_done, 8)
                        if gg == G_GA[1] and j == 0:
                            dve.wait_ge(lev_qe, 28)
                        take(gates[k][:, j], s)
                if g == G_G:
                    if j == 0:
                        dve.wait_ge(z_done, 8)
                    take(hg_g[:, j], s)

                if GROUPS[g][0] == "br":
                    branch, half = GROUPS[g][1]
                    d = 4 * half + j
                    dve.wait_ge(gate_ready, 2 * branch + half + 1)
                    gate = gates[2 * branch + half][:, j]
                    dve.wait_ge(tile_done, s + 1)
                    if branch == 0:
                        mark(v.tensor_tensor(merged[d], ps, gate, ALU.mult), dve_free)
                    else:
                        if d >= 2 or branch == 2:
                            dve.wait_ge(merged_sum, 8 * (branch - 1) + d - 1)
                        mark(v.tensor_tensor(br_t[d % 2], ps, gate, ALU.mult), dve_free)
                    if branch == 2 and d >= 2:
                        merged_rest(d - 2)

                for a in range(8):
                    if s == ATT_SP[a]:
                        dve.wait_ge(sp_ln, a + 1)
                        mark(v.scalar_tensor_tensor(stick[a % 2], pz[:, 0:1280], 0.0, stick[a % 2],
                                                    ALU.max, ALU.add), sp_ready)
                for a in range(1, 8, 2):
                    if s == ATT_S[a]:
                        dve.wait_ge(yb_hi, a // 2 + 1)
                        mark(v.tensor_tensor(ylo[:, 4 + a // 2], pyb, yhi[:, 4 + a // 2].bitcast(F32), ALU.subtract), yb_lo)

                if s == ON_AT + 1:
                    dve.wait_ge(on_a, 1)
                    dve.wait_ge(hgain_in, 16)
                    step(v.reciprocal(hg_rstd[:], hg_ss[:]))
                    after()
                if s in (ON_AT + 1, ON_AT + 2):
                    for i in range(8 * (s - ON_AT - 1), 8 * (s - ON_AT)):
                        t, h = divmod(i, 4)
                        o = hg_v[:, t, h * P:(h + 1) * P]
                        mark(v.scalar_tensor_tensor(o, o, hg_rstd[:, i:i + 1], hgain, ALU.mult, ALU.mult), on_d)
                t = s - YC_AT + 1
                if 0 <= t < 4:
                    if t == 0:
                        dve.wait_ge(g_ready, 1)
                        dve.wait_ge(on_d, 16)
                    mark(v.tensor_tensor(hg_v[:, t], hg_v[:, t], hg_g[:, t], ALU.mult), oc_ready)
                if s == 4 * G_OUT[0]:
                    merged_rest(6)
                    merged_rest(7)
                for t in range(4):
                    if s == YC_AT + t:
                        dve.wait_ge(yc_hi, t + 1)
                        mark(v.tensor_tensor(ylo[:, 0:4, t * P:(t + 1) * P],
                                             pside[:, t % 2].rearrange("p (a b) -> p a b", b=P),
                                             yhi[:, 0:4, t * P:(t + 1) * P].bitcast(F32), ALU.subtract), yc_lo)

                if g == G_OUT[0]:
                    half_to_mean(j, j + 1)
                    if j == 0:
                        dve.wait_ge(gain1_in, 16)
                    step(v.tensor_tensor(o4[:, j, 0:512], o4[:, j, 0:512], gain1[:, 0:512], ALU.mult))
                if g == G_OUT[1]:
                    if j == 0:
                        dve.wait_ge(gains_in, 32)
                        dve.wait_ge(x_again, 64)
                    if j == 2:
                        dve.wait_ge(h_hi, 5)
                        rest_t(yhi, ylo, 0, 0)
                    if j == 3:
                        second_norm(2, 11)
                    first_norm(j, (5, 7, 9, 10)[j])
                    if j != 2:
                        second_norm(j, (6, 8, None, 12)[j])

            for t in (2, 3):
                dve.wait_ge(h_hi, 4 + t + 1)
                rest_t(yhi, ylo, t, 2 * (t % 2))

            def mlp(f, g):
                if g == 2:
                    dve.wait_ge(sum_zero, 1)
                for j in range(4):
                    k = 4 * g + j
                    if f is not LAST or g < 3:
                        split_lo_mlp(rnd(f), k + 4)
                    if g < 2:
                        dve.wait_ge(relu_done, 8 * rnd(f) + (k + 1))
                        if k >= 2:
                            dve.wait_ge(hid_lo, 8 * rnd(f) + (k - 1))
                        v.scalar_tensor_tensor(hid[k % 2], mlp_tile(f, k), 0.0, relu[k % 2],
                                               ALU.max, ALU.mult).then_inc(hid_done, 1)
                        dve.wait_ge(hid_hi, 8 * rnd(f) + (k + 1))
                        v.tensor_tensor(hlo[:, k], hid[k % 2], hhi[:, k].bitcast(F32), ALU.subtract).then_inc(hid_lo, 1)
                    else:
                        half = g - 2
                        part = o4[:, j, 512 * half:512 * half + 512]
                        dve.wait_ge(tile_done, 16 * rnd(f) + (NS + k + 1))
                        v.tensor_tensor(part, part, mlp_tile(f, k), ALU.add).then_inc(dve_free, 1)
                        if f is LAST and half == 0:
                            half_to_mean(j, 4 + j + 1)
                            step(v.tensor_tensor(part, part, gain3[:, 0:512], ALU.mult))
                        if f is LAST and half == 1:
                            dve.wait_ge(dve_free, DVE_FREE0 + 8 * (NF - 1) + 4 + j + 1)
                            step(v.tensor_tensor(o_gain, part, gain3[:, 512:1024], ALU.mult))
                            dve.wait_ge(rms_done, 12 + j + 1)
                            step(v.reciprocal(rstd[:, j:j + 1], ss[:, j:j + 1]))
                            after()
                            for c, scaled in ((slice(0, 512), o4[:, j, 0:512]), (slice(512, 1024), o_gain)):
                                mark(v.scalar_tensor_tensor(o4[:, j, c], scaled, rstd[:, j:j + 1], x1[:, j, c],
                                                            ALU.mult, ALU.add), y_done)

            mlp(0, 0)
            with dve.Fori(0, NF - 1) as f:
                for g in (1, 2, 3):
                    mlp(f, g)
                mlp(f + 1, 0)
            for g in (1, 2, 3):
                mlp(LAST, g)

        @block.tensor
        def _(pe):
            mm = nc.tensor.matmul

            def product(dst, left, right, k, last_k):
                mm(dst, left[0], right[0], start=(k == 0), stop=False)
                mm(dst, left[0], right[1], start=False, stop=False)
                return mm(dst, left[1], right[0], start=False, stop=(k == last_k))

            def ring(U0, k):
                U = (U0 + k // 2) % RING
                return whi[:, U, k % 2], wlo[:, U, k % 2]

            def transposes(src, dst_bank, nk):
                for k in range(nk):
                    last = nc.tensor.transpose(pside[:, dst_bank + k // 4, (k % 4) * P:(k % 4 + 1) * P],
                                               src[:, k * P:(k + 1) * P], ident[:])
                return last

            pe.wait_ge(const_ready, 1)
            def h_tile(t):
                pe.wait_ge(xn_ready, t + 1)
                if t >= 2:
                    pe.wait_ge(h_lo, t - 1)
                transposes(xn[t % 2], 2 * (t % 2), 8).then_inc(xn_t, 1)

            def main(s):
                g, j = divmod(s, 4)
                kind = GROUPS[g][0]
                if s >= 2:
                    pe.wait_ge(*free_count(s - 2))
                dst = pmain[:, s % 2]
                nk = 4 if kind == "br" else 8
                y0 = 0 if kind != "br" else (0, 4, 0)[GROUPS[g][1][0]]
                for k in range(nk):
                    if j == 0 and k % 2 == 0:
                        pe.wait_ge(w_lo, FIRST_UNIT[g] + k // 2 + 1)
                    if kind == "out" and s == 4 * G_OUT[0]:
                        pe.wait_ge(merged_lo, k + 1)
                    w = ring(FIRST_UNIT[g], k)
                    if kind in ("feat", "br"):
                        left = tuple(x[:, j * P:(j + 1) * P] for x in w)
                        right = (hhi[:, k], hlo[:, k]) if kind == "feat" else (yhi[:, y0 + k], ylo[:, y0 + k])
                    else:
                        left = (hhi[:, k, j * P:(j + 1) * P], hlo[:, k, j * P:(j + 1) * P])
                        right = w
                    if s < 3 and k == (5 if s == 0 else 3):
                        h_tile(s + 1)
                    if s >= NS - 2 and k == 4:
                        h2_tile(s - (NS - 2))
                    if s in ATT_S and k == 2:
                        att_suffix(ATT_S.index(s))
                    last = product(dst, left, right, k, nk - 1)
                last.then_inc(tile_done, 1)

            def rg_gates(j):
                pe.wait_ge(rg_conv, j + 1)
                if j == 0:
                    pe.wait_ge(rgw_in, 64)
                    pe.wait_ge(par_ready, 1)
                else:
                    pe.wait_ge(rg_sig, 2 * j)
                mm(ph[0], rg_wa[:, j], rg_xc[:, j], start=True, stop=True)
                mm(ph[1], rg_wx[:, j], rg_xc[:, j], start=True, stop=True).then_inc(rg_gate, 1)

            def levels(h, p):
                for i in range(2):
                    r = 2 * p + i
                    if r == 7:
                        pe.wait_ge(lev_ke, 7 * h + 7)
                        if h:
                            pe.wait_ge(kd_ready, 2 * h)
                        transposes(lev_k[1], 0, 4).then_inc(kd_t, 1)
                        continue
                    if r == 0:
                        pe.wait_ge(b_ready, h + 1)
                        pe.wait_ge(f_k, h + 1)
                        pe.wait_ge(*free_count(4 * G_Q + 3))
                        kk, qq = hg_k[:, h], hg_q[:, h]
                    else:
                        pe.wait_ge(lev_ke, 7 * h + r)
                        pe.wait_ge(lev_qe, 7 * h + r)
                        kk, qq = lev_k[i], lev_q[i]
                    if h == 0 and r < 2:
                        pe.wait_ge(rg_sig, 8)
                    else:
                        pe.wait_ge(lev_m, 7 * h + max(r - 1, 0))
                    for t in range(4):
                        c = slice(t * P, (t + 1) * P)
                        dst, tok = ph[i][:, c], qq[:, c]
                        if r:
                            dst, tok = (halves(b, LEVELS[r - 1])[1] for b in (dst, tok))
                        last = mm(dst, kk[:, c], tok, start=True, stop=True)
                    last.then_inc(lev_p, 1)

            def chunk_products(h):
                pe.wait_ge(lev_m, 7 * (h + 1))
                pe.wait_ge(kd_ready, 2 * h + 2)
                if h:
                    pe.wait_ge(o_ready, h)
                    pe.wait_ge(st_ready, 7 * h)
                else:
                    pe.wait_ge(act_free, free_count(4 * G_I + 3)[1])
                for t in range(4):
                    mm(pyb[:, t * P:(t + 1) * P], attn_t[:, t], hg_v[:, t, h * P:(h + 1) * P],
                       start=(t == 0), stop=False, skip_group_check=True)
                for c in range(7):
                    rows = slice(64 * (c % 2), 64 * (c % 2) + 64)
                    last = mm(pside[:, 1 + c % 2, (c // 2) * P:(c // 2 + 1) * P], kdt[rows, c // 2],
                              hg_v[rows, c // 2, h * P:(h + 1) * P], start=True, stop=True)
                last.then_inc(kv_done, 1)

            def state_products(h):
                pe.wait_ge(st_ready, 7 * (h + 1))
                pe.wait_ge(lev_qe, 7 * (h + 1))
                for c in range(1, 8):
                    rows = slice(64 * (c % 2), 64 * (c % 2) + 64)
                    last = mm(pyb[rows, (c // 2) * P:(c // 2 + 1) * P], qb[:, 64 * c:64 * c + 64],
                              states[:, c - 1], start=False, stop=(c == 7), skip_group_check=True)
                last.then_inc(o_done, 1)


            def att_z(a):
                rows = slice(64 * (a % 2), 64 * (a % 2) + 64)
                if a == 0:
                    pe.wait_ge(act_free, free_count(4 * G_SV + 3)[1])
                    pe.wait_ge(st_ready, 28)
                    pe.wait_ge(kd_ready, 8)
                else:
                    pe.wait_ge(w_exp, a)
                for b in (0, 1, 3, 2):
                    last = mm(pz[:, Z_AT[b]:Z_AT[b] + S - P * b], sb_k[rows, a // 2, b * P:(b + 1) * P],
                              sb_q[rows, a // 2, b * P:S], start=(b != 3), stop=False, skip_group_check=True)
                last.then_inc(z_done, 1)

            def att_suffix(a):
                pe.wait_ge(sp_masked, a + 1)
                sp_ = stick[a % 2]

                def add(left, at_z, right, stop):
                    return mm(pz[:, at_z:at_z + right.shape[-1]], left, right, start=False, stop=stop,
                              skip_group_check=True)

                for b in range(4):
                    add(ntri[:], Z_AT[b], sp_[:, Z_AT[b]:Z_AT[b] + S - P * b], b == 3)
                for b in range(3):
                    add(nones[:], Z_AT[b] + P, sp_[:, Z_AT[b + 1]:Z_AT[b + 1] + P], b == 2)
                pe.wait_ge(summed, a + 1)
                add(nones[:], Z_AT[0] + 2 * P, key_sums[:, 0:2 * P], True)
                add(nones[:], Z_AT[1] + 2 * P, key_sums[:, 2 * P:3 * P], True).then_inc(suf_done, 1)

            def att_out(a):
                pe.wait_ge(w_ready, a + 1)
                if a == 0:
                    pe.wait_ge(o_ready, 4)
                elif a % 2 == 0:
                    pe.wait_ge(yb_lo, a // 2)
                rows = slice(64 * (a % 2), 64 * (a % 2) + 64)
                for b in range(4):
                    last = mm(pyb[rows, b * P:S], sb_v[:, b, 64 * a:64 * a + 64],
                              stick[a % 2][:, Z_AT[b]:Z_AT[b] + S - P * b],
                              start=(b == 0), stop=(b == 3), skip_group_check=True)
                last.then_inc(av_done, 1)

            def h2_tile(t):
                pe.wait_ge(xn_ready, 4 + t + 1)
                if t >= 2:
                    pe.wait_ge(h_lo, 4 + t - 1)
                transposes(o4[:, t], 2 * (t % 2), 8).then_inc(xn_t, 1)

            for s in range(NS):
                if s == 4 * 8:
                    pe.wait_ge(ya_lo, 1)
                if GROUPS[s // 4] == ("br", (1, 0)) and s % 4 == 0:
                    pe.wait_ge(yb_lo, 4)
                if s == 4 * 18:
                    pe.wait_ge(yc_lo, 4)
                if s == 0:
                    h_tile(0)
                if s < 4:
                    if s == 3:
                        pe.wait_ge(par_in, 96)
                        nc.tensor.transpose(ph[0][:, 0:NPAR], par_rows[0:NPAR, :],
                                            ident[0:NPAR, 0:NPAR]).then_inc(par_t, 1)
                    pe.wait_ge(h_lo, s + 1)
                main(s)
                if RG_AT + 2 <= s < RG_AT + 6:
                    rg_gates(s - RG_AT - 2)
                for h, b in enumerate(HG_AT):
                    if s == b + 4:
                        chunk_products(h)
                for h, b in enumerate(HG_AT):
                    if b <= s < b + 4:
                        levels(h, s - b)
                    if s == HG_OUT[h]:
                        state_products(h)
                if s in ATT_Z:
                    att_z(ATT_Z.index(s))
                if s in ATT_S:
                    att_out(ATT_S.index(s))
                for t in range(4):
                    if s == YC_AT + t:
                        pe.wait_ge(oc_ready, t + 1)
                        if t >= 2:
                            pe.wait_ge(yc_lo, t - 1)
                        transposes(hg_v[:, t], t % 2, 4).then_inc(oc_t, 1)

            def mlp(f, g):
                for j in range(4):
                    k = 4 * g + j
                    if k in (0, 1):
                        pe.wait_ge(dve_free, 8 * rnd(f) + (DVE_FREE0 - 1 + k))
                    elif k < 10:
                        pe.wait_ge(hid_done, 8 * rnd(f) + (k - 1))
                    else:
                        pe.wait_ge(dve_free, 8 * rnd(f) + (DVE_FREE0 + k - 9))
                    dst = mlp_tile(f, k)
                    for kt in range(8):
                        if j == 0 and kt % 2 == 0:
                            pe.wait_ge(w_lo, 16 * rnd(f) + (NU + 4 * g + kt // 2 + 1))
                        if k == 8:
                            pe.wait_ge(hid_lo, 8 * rnd(f) + (kt + 1))
                        w = ring(NU + 4 * g, kt)
                        if g < 2:
                            last = product(dst, tuple(x[:, j * P:(j + 1) * P] for x in w),
                                           (yhi[:, kt], ylo[:, kt]), kt, 7)
                        else:
                            last = product(dst, (hhi[:, kt, j * P:(j + 1) * P], hlo[:, kt, j * P:(j + 1) * P]),
                                           w, kt, 7)
                    last.then_inc(tile_done, 1)

            pe.wait_ge(*free_count(NS - 1))
            pe.wait_ge(*free_count(NS - 2))
            for half in range(2):
                pe.wait_ge(h_lo, 6 + 2 * half)
                tok = slice(256 * half, 256 * half + 256)
                for j in range(4):
                    for kt in range(8):
                        if half == 0 and j == 0 and kt % 2 == 0:
                            pe.wait_ge(w_lo, NU + kt // 2 + 1)
                        last = product(mlp_tile(0, j)[:, tok], tuple(x[:, j * P:(j + 1) * P] for x in ring(NU, kt)),
                                       (yhi[:, kt, tok], ylo[:, kt, tok]), kt, 7)
                    if half:
                        last.then_inc(tile_done, 1)
                    elif j in (1, 2):
                        h2_tile(j + 1)

            with pe.Fori(0, NF - 1) as f:
                for g in (1, 2, 3):
                    mlp(f, g)
                mlp(f + 1, 0)
            for g in (1, 2, 3):
                mlp(LAST, g)


_INS = ["x", "ln_gains", "w_in", "conv_w", "conv_b", "rg_w_a", "rg_b_a", "rg_w_x", "rg_b_x", "rg_lambda",
        "lb_logits", "hgrn_norm", "w_branch", "w_out", "w_up", "w_down"]


def kernel(**inputs):
    import numpy as _np
    import concourse.bacc as _bacc
    from concourse import mybir as _mybir
    from concourse.bass_utils import run_bass_kernel_spmd as _run

    nc = _bacc.Bacc("TRN2", target_bir_lowering=False, num_devices=1, dynamic_dma_scratch_size=1024)
    arrays, args = {}, []
    for name in _INS:
        a = _np.ascontiguousarray(inputs[name])
        arrays[f"in_{name}"] = a
        args.append(nc.dram_tensor(f"in_{name}", a.shape, _mybir.dt.from_np(a.dtype), kind="ExternalInput").ap())
    shape = inputs["x"].shape
    args.append(nc.dram_tensor("out_x", shape, _mybir.dt.float32, kind="ExternalOutput").ap())
    trunk(nc, *args)
    r = _run(nc, [arrays], core_ids=[0])
    return r.results[0]["out_x"]
```
